# Optimizing a Trainium2 kernel written in Bass

```python
import math
import jax, jax.numpy as jnp
from jax import lax
import numpy as np

D_MODEL = 1024
BATCH = 1
SEQ = 512
DEPTH = 2

N_A_LAYERS = DEPTH // 2
N_B_LAYERS = DEPTH - N_A_LAYERS
S5_GROUP = 16
S5_GROUPS = D_MODEL // S5_GROUP
S5_STATE = 64
DT_MIN = 1e-3
DT_MAX = 1e-1
LAMBDA_RE_MAX = -1e-4
HEAD_DIM = 64
N_Q_HEADS = D_MODEL // HEAD_DIM
N_KV_HEADS = 4
Q_PER_KV = N_Q_HEADS // N_KV_HEADS
WINDOW = 128
BLOCK = 128
D_FF = 4 * D_MODEL
NORM_EPS = 1e-5

kernel_name = "yoco_s5_swa_sink_hybrid"

def rmsnorm(x, g):
    x32 = x.astype(jnp.float32)
    y = x32 * lax.rsqrt(jnp.mean(x32 * x32, axis=-1, keepdims=True) + NORM_EPS)
    return (y * g.astype(jnp.float32)).astype(x.dtype)

def s5_mixer(u, a_re, a_im, log_dt, b_re, b_im, c_re, c_im, d_skip, w_glu, b_glu):
    bsz, seq, _ = u.shape
    f32 = jnp.float32
    u32 = u.astype(f32)
    ug = u32.reshape(bsz, seq, S5_GROUPS, S5_GROUP)
    lam = lax.complex(jnp.minimum(a_re.astype(f32), LAMBDA_RE_MAX), a_im.astype(f32))
    dt = jnp.exp(log_dt.astype(f32))[:, None]
    lam_bar = jnp.exp(lam * dt)
    b_c = lax.complex(b_re.astype(f32), b_im.astype(f32))
    b_bar = ((lam_bar - 1.0) / lam)[:, :, None] * b_c
    bu = lax.complex(jnp.einsum('blgc,gpc->blgp', ug, jnp.real(b_bar)),
                     jnp.einsum('blgc,gpc->blgp', ug, jnp.imag(b_bar)))
    a = jnp.broadcast_to(lam_bar[None, None], (1, seq, S5_GROUPS, S5_STATE))

    def combine(left, right):
        a_l, b_l = left
        a_r, b_r = right
        return a_r * a_l, a_r * b_l + b_r

    _, states = lax.associative_scan(combine, (a, bu), axis=1)
    y = (jnp.einsum('blgp,gcp->blgc', jnp.real(states), c_re.astype(f32))
         - jnp.einsum('blgp,gcp->blgc', jnp.imag(states), c_im.astype(f32)))
    y = y.reshape(bsz, seq, D_MODEL) + d_skip.astype(f32) * u32
    y = jax.nn.gelu(y).astype(u.dtype)
    z = y @ w_glu + b_glu
    val, gate = jnp.split(z, 2, axis=-1)
    return val * jax.nn.sigmoid(gate)

def shared_kv(h, g_kv, w_kv, b_kv):
    bsz, seq, _ = h.shape
    kv = rmsnorm(h, g_kv) @ w_kv + b_kv
    k, v = jnp.split(kv, 2, axis=-1)
    return (k.reshape(bsz, seq, N_KV_HEADS, HEAD_DIM),
            v.reshape(bsz, seq, N_KV_HEADS, HEAD_DIM))

def window_blocks(t, nb):
    bsz = t.shape[0]
    tb = t.reshape(bsz, nb, BLOCK, N_KV_HEADS, HEAD_DIM)
    prev = jnp.concatenate([jnp.zeros_like(tb[:, :1]), tb[:, :-1]], axis=1)
    return jnp.moveaxis(jnp.concatenate([prev, tb], axis=2), 1, 0)

def swa_sink_attention(hn, k, v, w_q, b_q, sinks, w_o, b_o):
    bsz, seq, _ = hn.shape
    nb = seq // BLOCK
    f32 = jnp.float32
    scale = 1.0 / math.sqrt(HEAD_DIM)
    q = (hn @ w_q + b_q).reshape(bsz, nb, BLOCK, N_KV_HEADS, Q_PER_KV, HEAD_DIM)
    q = jnp.moveaxis(q, 1, 0)
    kw = window_blocks(k, nb)
    vw = window_blocks(v, nb)
    qi = jnp.arange(BLOCK)[:, None]
    kj = jnp.arange(2 * BLOCK)[None, :]
    diff = qi + BLOCK - kj
    band = (diff >= 0) & (diff < WINDOW)
    sink = sinks.astype(f32).reshape(N_KV_HEADS, Q_PER_KV)[None, :, :, None]

    def block_fn(args):
        n, qb, kb, vb = args
        s = jnp.einsum('bqkgd,bskd->bkgqs', qb.astype(f32), kb.astype(f32)) * scale
        valid = band & ((n - 1) * BLOCK + kj >= 0)
        s = jnp.where(valid, s, -jnp.inf)
        m = jnp.maximum(jnp.max(s, axis=-1), sink)
        p = jnp.exp(s - m[..., None])
        denom = jnp.sum(p, axis=-1) + jnp.exp(sink - m)
        o = jnp.einsum('bkgqs,bskd->bqkgd', p / denom[..., None], vb.astype(f32))
        return o.astype(hn.dtype)

    o = lax.map(block_fn, (jnp.arange(nb), q, kw, vw))
    o = jnp.moveaxis(o, 0, 1).reshape(bsz, seq, N_Q_HEADS * HEAD_DIM)
    return o @ w_o + b_o

def sq_relu_mlp(h, w_in, w_out):
    return jnp.square(jax.nn.relu(h @ w_in)) @ w_out

def setup_inputs(seed: int = 0) -> dict:
    key = jax.random.key(seed)
    ks = jax.random.split(key, 26)
    f32 = jnp.float32
    nrm = lambda k, shape, s: jax.random.normal(k, shape, f32) * s
    G, P, GC, D = S5_GROUPS, S5_STATE, S5_GROUP, D_MODEL
    HQ = N_Q_HEADS * HEAD_DIM
    HKV = N_KV_HEADS * HEAD_DIM
    x = jax.random.normal(ks[0], (BATCH, SEQ, D), f32)
    norm_mix = 1.0 + nrm(ks[1], (DEPTH, D), 0.02)
    norm_mlp = 1.0 + nrm(ks[2], (DEPTH, D), 0.02)
    norm_kv = 1.0 + nrm(ks[3], (D,), 0.02)
    norm_final = 1.0 + nrm(ks[4], (D,), 0.02)
    s5_a_re = -0.5 + nrm(ks[5], (N_A_LAYERS, G, P), 0.01)
    s5_a_im = (jnp.pi * jnp.arange(P, dtype=f32))[None, None, :] + nrm(ks[6], (N_A_LAYERS, G, P), 0.01)
    s5_log_dt = jax.random.uniform(ks[7], (N_A_LAYERS, G), f32, math.log(DT_MIN), math.log(DT_MAX))
    s5_b_re = nrm(ks[8], (N_A_LAYERS, G, P, GC), (2.0 * GC) ** -0.5)
    s5_b_im = nrm(ks[9], (N_A_LAYERS, G, P, GC), (2.0 * GC) ** -0.5)
    s5_c_re = nrm(ks[10], (N_A_LAYERS, G, GC, P), P ** -0.5)
    s5_c_im = nrm(ks[11], (N_A_LAYERS, G, GC, P), P ** -0.5)
    s5_d = nrm(ks[12], (N_A_LAYERS, D), 1.0)
    s5_w_glu = nrm(ks[13], (N_A_LAYERS, D, 2 * D), D ** -0.5)
    s5_b_glu = nrm(ks[14], (N_A_LAYERS, 2 * D), 0.01)
    w_kv = nrm(ks[15], (D, 2 * HKV), D ** -0.5)
    b_kv = nrm(ks[16], (2 * HKV,), 0.01)
    w_q = nrm(ks[17], (N_B_LAYERS, D, HQ), D ** -0.5)
    b_q = nrm(ks[18], (N_B_LAYERS, HQ), 0.01)
    sinks = nrm(ks[19], (N_B_LAYERS, N_Q_HEADS), 0.5)
    w_o = nrm(ks[20], (N_B_LAYERS, HQ, D), HQ ** -0.5)
    b_o = nrm(ks[21], (N_B_LAYERS, D), 0.01)
    w_mlp_in = nrm(ks[22], (DEPTH, D, D_FF), D ** -0.5)
    w_mlp_out = nrm(ks[23], (DEPTH, D_FF, D), D_FF ** -0.5)
    return {"x": x, "norm_mix": norm_mix, "norm_mlp": norm_mlp, "norm_kv": norm_kv,
            "norm_final": norm_final, "s5_a_re": s5_a_re, "s5_a_im": s5_a_im,
            "s5_log_dt": s5_log_dt, "s5_b_re": s5_b_re, "s5_b_im": s5_b_im,
            "s5_c_re": s5_c_re, "s5_c_im": s5_c_im, "s5_d": s5_d, "s5_w_glu": s5_w_glu,
            "s5_b_glu": s5_b_glu, "w_kv": w_kv, "b_kv": b_kv, "w_q": w_q, "b_q": b_q,
            "sinks": sinks, "w_o": w_o, "b_o": b_o, "w_mlp_in": w_mlp_in,
            "w_mlp_out": w_mlp_out}

def reference(x, norm_mix, norm_mlp, norm_kv, norm_final, s5_a_re, s5_a_im, s5_log_dt,
              s5_b_re, s5_b_im, s5_c_re, s5_c_im, s5_d, s5_w_glu, s5_b_glu, w_kv, b_kv,
              w_q, b_q, sinks, w_o, b_o, w_mlp_in, w_mlp_out):
    h = x
    k = v = None
    for layer in range(DEPTH):
        if layer < N_A_LAYERS:
            hn = rmsnorm(h, norm_mix[layer])
            h = h + s5_mixer(hn, s5_a_re[layer], s5_a_im[layer], s5_log_dt[layer],
                             s5_b_re[layer], s5_b_im[layer], s5_c_re[layer], s5_c_im[layer],
                             s5_d[layer], s5_w_glu[layer], s5_b_glu[layer])
        else:
            if layer == N_A_LAYERS:
                k, v = shared_kv(h, norm_kv, w_kv, b_kv)
            bi = layer - N_A_LAYERS
            hn = rmsnorm(h, norm_mix[layer])
            h = h + swa_sink_attention(hn, k, v, w_q[bi], b_q[bi], sinks[bi], w_o[bi], b_o[bi])
        h = h + sq_relu_mlp(rmsnorm(h, norm_mlp[layer]), w_mlp_in[layer], w_mlp_out[layer])
    return rmsnorm(h, norm_final)


_drawn_inputs = setup_inputs


def setup_inputs(seed=0):
    import zlib

    import numpy as np

    out = dict(_drawn_inputs(seed))
    spreads = {}
    factors = {'norm_mix': 6.371,
     'norm_kv': 8.0,
     'norm_final': 8.074,
     's5_a_re': 64.0,
     's5_b_glu': 8.0,
     'b_kv': 46.775,
     'b_q': 8.0,
     'sinks': 64.0,
     'b_o': 46.278}
    for name, (base, spread) in spreads.items():
        noise = np.random.default_rng([zlib.crc32(name.encode()), seed]).standard_normal(out[name].shape)
        drawn = base * np.exp(spread * noise) if base else spread * noise
        out[name] = __import__('jax').numpy.asarray(drawn.astype(out[name].dtype))
    for name, factor in factors.items():
        out[name] = (out[name] * factor).astype(out[name].dtype)
    return out
```

```python
from contextlib import ExitStack

import numpy as np

import concourse.bass as bass
from concourse import mybir

F32 = mybir.dt.float32
F32R = mybir.dt.float32r
ALU = mybir.AluOpType
ACT = mybir.ActivationFunctionType
AX = mybir.AxisListType

P = 128
D = 1024
L = 512
KT = D // P
FF = 4 * D
NB_FF = FF // D
EPS = 1e-5
J = 8
NK = L // J
C = 16
G = D // C
S = 64
GP = G // 2
OCT = 8
NO = G // OCT
OGP = OCT // 2
HD = 64
NQ = 16
NKV = 4
BLK = 128
NBLK = L // BLK
QUADS = 4
LAM_MAX = -1e-4

U_GLU = 0
U_MLP = (U_GLU + 2 * KT, U_GLU + 2 * KT + 2 * NB_FF * KT + 4 + 2 * KT)
U_KV = U_MLP[0] + 2 * NB_FF * KT
U_Q = U_KV + 4
U_O = U_Q + KT
NU = U_MLP[1] + 2 * NB_FF * KT
assert U_O + KT == U_MLP[1] and U_GLU == 0

PRM = {}
_at = 0
for _name, _n in (("a_re", GP), ("a_im", GP), ("log_dt", GP), ("b_re", GP * C), ("b_im", GP * C),
                  ("c_re", GP * C), ("c_im", GP * C), ("g_in", G)):
    PRM[_name] = (_at, _at + _n)
    _at += _n
N_PRM = _at
NPOW = (J + 1) + J
CST = {}
_at = 0
for _name, _n in (("pow", NPOW), ("chunk", NK), ("keep", NK), ("same_step", P), ("ident", P), ("ones", P)):
    CST[_name] = (_at, _at + _n)
    _at += _n
N_CST = _at
COL = {}
_at = 0
for _name, _n in (("b_val", KT), ("b_gate", KT), ("g_mlp0", KT), ("g_kv", KT), ("g_q", KT), ("g_mlp1", KT),
                  ("g_out", KT), ("b_k", 2), ("b_q", KT), ("b_o", KT), ("b_v", NKV * HD), ("sink", NQ)):
    COL[_name] = (_at, _at + _n)
    _at += _n
N_COL = _at

H_MLP = (KT, KT + NB_FF * KT + KT)
H_O = KT + NB_FF * KT
SETUP_EXP, SETUP_PH, SETUP_POW, SETUP_TAB, SETUP_MS = 4, 10, 25, 43, 66
STAT_A = (1, 3, 4, 5)

TWO_PI = 6.283185
PI_ = 3.1415925
ROUND = 1.5 * 2.0 ** 23


def build(nc, panels, xu_d, x_d, prm_d, ddiag_d, cst_d, mask_d, col_d, out_d):
    ctx = ExitStack()
    with ctx:
        y_dram = nc.dram_tensor("y_scratch", (G, C, J, NK), F32, kind="Internal").ap()

        def sb(name, shape, dt=F32, where=ctx):
            return where.enter_context(nc.sbuf_tensor(name, shape, dt))

        def sem(name):
            return ctx.enter_context(nc.semaphore(name))

        h = sb("h", [P, KT, L])
        raw = sb("raw", [P, 2, D])
        w_hi = sb("w_hi", [P, 4, D], F32R)
        w_lo = sb("w_lo", [P, 4, D], F32R)
        cst = sb("cst", [P, N_CST])
        col = sb("col", [P, N_COL])
        acc = sb("acc", [P, L])
        rstd = sb("rstd", [P, L])
        rcol = sb("rcol", [P, NBLK])
        stat = sb("stat", [P, L])
        scol = sb("scol", [P, NBLK])
        gate_sb = sb("gate_sb", [P, 2])
        t1 = sb("t1", [P, L])
        t2 = sb("t2", [P, 2, L])

        s5 = ExitStack()
        prm = sb("prm", [P, N_PRM], where=s5)
        ddiag = sb("ddiag", [C, 2, GP, C], where=s5)
        small = sb("small", [P, 16, GP], where=s5)
        ph = sb("ph", [P, GP, NPOW], where=s5)
        mag = sb("mag", [P, GP, NPOW], where=s5)
        rnd = sb("rnd", [P, GP, NPOW], where=s5)
        l_im = sb("l_im", [P, GP, NPOW], where=s5)
        l_re = sb("l_re", [P, GP, NPOW], where=s5)
        nl_re = sb("nl_re", [P, GP, J + 1], where=s5)
        nl_im = sb("nl_im", [P, GP, J + 1], where=s5)
        x_re = sb("x_re", [P, GP, J], where=s5)
        x_im = sb("x_im", [P, GP, J], where=s5)
        cosk = sb("cosk", [P, GP, NK], where=s5)
        sink_ = sb("sink_", [P, GP, NK], where=s5)
        phk = sb("phk", [P, 8, NK], where=s5)
        phr = sb("phr", [P, 8, NK], where=s5)
        rstd_u = sb("rstd_u", [P, 2, NK], where=s5)
        p_tmp = sb("p_tmp", [P, 2, OGP, J, C], where=s5)
        p_ri = sb("p_ri", [P, 2, 2, OGP, J, C], where=s5)
        w_tmp = sb("w_tmp", [P, 2, OGP, J + 1, C], where=s5)
        w_ri = sb("w_ri", [P, 2, 2, OGP, J + 1, C], where=s5)
        v_ri = sb("v_ri", [P, 2, 2, OGP, P], where=s5)
        k_out = sb("k_out", [C, 2, OGP, P], where=s5)
        toep = sb("toep", [P, 2, 2, OGP, P], where=s5)
        u_tmp = sb("u_tmp", [P, OCT, NK], where=s5)
        u_sb = sb("u_sb", [P, 2, OCT, NK], where=s5)
        decay = sb("decay", [P, 2, 2, OGP, NK], where=s5)
        rc = sb("rc", [P, 2, OGP, NK], where=s5)
        rs = sb("rs", [P, 2, OGP, NK], where=s5)
        rb = sb("rb", [P, 2, OGP, NK], where=s5)
        st = sb("st", [P, 2, 2, OGP, NK + 1], where=s5)
        y_sb = sb("y_sb", [P, 2, OCT * NK], where=s5)
        xy = sb("xy", [P, G, NK], where=s5)
        s5.close()

        hid = sb("hid", [P, 2, 2, KT, L], F32R)
        over = ExitStack()
        act = sb("act", [P, 2, KT, L], F32R, where=over)
        over.close()
        over = ExitStack()
        qT = sb("qT", [P, KT, L], where=over)
        qstage = sb("qstage", [P, 2, 4, BLK], where=over)
        pT = sb("pT", [P, 2, 4, 2, BLK], where=over)
        o_sb = sb("o_sb", [P, 2, 4, HD], where=over)
        fill = sb("fill", [P, 32 * 256 - (KT * L + 2 * 4 * BLK + 2 * 4 * 2 * BLK + 2 * 4 * HD)], where=over)
        kT = sb("kT", [P, 2, BLK + L], where=over)
        v_sb = sb("v_sb", [P, 1 + NBLK, NKV * HD], where=over)
        s_sb = sb("s_sb", [P, 2, 4, 2 * BLK], where=over)
        mask = sb("mask", [P, NBLK, 2 * BLK], where=over)
        mx = sb("mx", [P, 2, 4], where=over)
        negm = sb("negm", [P, 2, 4], where=over)
        sm = sb("sm", [P, 2, 4], where=over)
        es = sb("es", [P, 2, 4], where=over)
        den = sb("den", [P, 2, 4], where=over)
        rden = sb("rden", [P, 2, 4], where=over)
        over.close()

        ps = ctx.enter_context(nc.psum_tensor("ps", [P, 8, 512], F32))

        s_prm, s_cst, s_xu, s_h, s_col, s_mask, s_dd = (sem(n) for n in (
            "prm_in", "cst_in", "xu_in", "h_in", "col_in", "mask_in", "ddiag_in"))
        raw_in = [sem("raw_in0"), sem("raw_in1")]
        w_hi_done, w_split = sem("w_hi_done"), sem("w_split")
        unit_done, bank_free = sem("unit_done"), sem("bank_free")
        setup_v, setup_a = sem("setup_v"), sem("setup_a")
        sq_ready, sq_used = sem("sq_ready"), sem("sq_used")
        zeroed, passed = sem("zeroed"), sem("passed")
        p_step, p_done, u_step, u_done = sem("p_step"), sem("p_done"), sem("u_step"), sem("u_done")
        w_step, w_done = sem("w_step"), sem("w_done")
        t_mm, k_mm, b_mm, y_mm = sem("t_mm"), sem("k_mm"), sem("b_mm"), sem("y_mm")
        v_evac, k_evac, k_diag = sem("v_evac"), sem("k_evac"), sem("k_diag")
        b_read, rot, st_done = sem("b_read"), sem("rot"), sem("st_done")
        t_in = [sem("toep_in0"), sem("toep_in1")]
        gelu_done = sem("gelu_done")
        y_out = [sem("y_out0"), sem("y_out1")]
        y_back = [sem("y_back0"), sem("y_back1")]
        y_hi, y_lo = sem("y_hi"), sem("y_lo")
        sig_done, glu_val = sem("sig_done"), sem("glu_val")
        h_added, sq_tmp, sq_acc = sem("h_added"), sem("sq_tmp"), sem("sq_acc")
        n_hi, n_lo = sem("n_hi"), sem("n_lo")
        stat_mm, stat_v, stat_a = sem("stat_mm"), sem("stat_v"), sem("stat_a")
        stat_col_mm, stat_c = sem("stat_col_mm"), sem("stat_c")
        hid_t, hid_sq, hid_hi, hid_lo = sem("hid_t"), sem("hid_sq"), sem("hid_hi"), sem("hid_lo")
        kv_tmp, kv_done, pads = sem("kv_tmp"), sem("kv_done"), sem("pads")
        q_tmp, q_done = sem("q_tmp"), sem("q_done")
        q_staged, s_mm, s_masked, m_step = sem("q_staged"), sem("s_mm"), sem("s_masked"), sem("m_step")
        p_exp, es_done, den_done, rden_done = sem("p_exp"), sem("es_done"), sem("den_done"), sem("rden_done")
        pt_mm, pt_v, pt_a = sem("pt_mm"), sem("pt_v"), sem("pt_a")
        o_mm, o_norm, ot_mm, ot_hi, ot_lo = sem("o_mm"), sem("o_norm"), sem("ot_mm"), sem("ot_hi"), sem("ot_lo")
        out_t, out_s = sem("out_tile"), sem("out_stored")

        def wait(eng, s, value):
            if not (isinstance(value, int) and value <= 0):
                eng.wait_ge(s, value)

        def C_(name):
            a, b = CST[name]
            return cst[:, a:b]

        def COLS(name):
            a, b = COL[name]
            return col[:, a:b]

        def PR(name):
            a, b = PRM[name]
            return prm[:, a:b]

        def octets(eng, first, lagged):
            first(0, 0)
            first(1, 1)
            lagged(0, 0)
            with eng.Fori(1, NO // 2) as i:
                first(2 * i, 0)
                lagged(2 * i - 1, 1)
                first(2 * i + 1, 1)
                lagged(2 * i, 0)
            lagged(NO - 1, 1)

        ident, ones = C_("ident"), C_("ones")
        block = ctx.enter_context(nc.Block())

        @block.sync
        def _(sp):
            sp.dma_start(prm[:], prm_d).then_inc(s_prm, 16)
            sp.dma_start(cst[:], cst_d).then_inc(s_cst, 16)
            sp.dma_start(xy[:], xu_d).then_inc(s_xu, 16)
            sp.dma_start(ddiag[:], ddiag_d).then_inc(s_dd, 16)
            sp.dma_start(col[:], col_d).then_inc(s_col, 16)
            for s in range(2):
                sp.dma_start(raw[:, s, :], panels[s]).then_inc(raw_in[s], 16)
            sp.dma_start(h[:], x_d).then_inc(s_h, 16)

            def toeplitz(o, q):
                wait(sp, k_diag, o + 1)
                wait(sp, zeroed, 3)
                for j in range(J):
                    sp.dma_start(toep[j * C:(j + 1) * C, q, :, :, j * C:].rearrange("p e g n -> p (e g) n"),
                                 k_out[:, :, :, 0:(J - j) * C].rearrange("p e g n -> p (e g) n")
                                 ).then_inc(t_in[q], 16)

            def turn(o, q):
                wait(sp, gelu_done, o + 1)
                for j in range(J):
                    sp.dma_start(y_dram[bass.ds(o * OCT, OCT), :, j, :].rearrange("g c k -> c g k"),
                                 y_sb[j * C:(j + 1) * C, q, :].rearrange("c (g k) -> c g k", g=OCT)
                                 ).then_inc(y_out[q], 16)
                wait(sp, y_out[q], 16 * J * (o // 2 + 1))
                sp.dma_start(xy[:, bass.ds(o * OCT, OCT), :].rearrange("p g k -> p (g k)"),
                             y_dram[bass.ds(o * OCT, OCT)].rearrange("g c j k -> (g c) (j k)")
                             ).then_inc(y_back[q], 16)

            octets(sp, toeplitz, turn)

            for u in (2, 3):
                wait(sp, w_split, u - 1)
                sp.dma_start(raw[:, u % 2, :], panels[u]).then_inc(raw_in[u % 2], 16)
            wait(sp, y_lo, KT)
            sp.dma_start(mask[:], mask_d).then_inc(s_mask, 16)
            with sp.Fori(2, NU // 2) as i:
                for s in range(2):
                    sp.wait_ge(w_split, 2 * i + s - 1)
                    sp.sem_inc(passed, 1)
                    sp.wait_ge(unit_done, 2 * i + s - 3)
                    sp.sem_inc(passed, 1)
                    sp.dma_start(raw[:, s, :], panels[2 * i + s]).then_inc(raw_in[s], 16)
            for m in range(KT):
                wait(sp, out_t, m + 1)
                sp.dma_start(out_d[m], h[:, m, :]).then_inc(out_s, 16)
            sp.wait_ge(out_s, 16 * KT)

        @block.gpsimd
        def _(pool):
            def gate():
                nc.gpsimd.tensor_tensor(gate_sb[:, 0:1], gate_sb[:, 1:2], gate_sb[:, 1:2], ALU.mult)

            nc.gpsimd.memset(gate_sb[:], 0.0).then_inc(zeroed, 1)
            wait(pool, zeroed, 1)

            nc.gpsimd.memset(st[:], 0.0).then_inc(zeroed, 1)
            nc.gpsimd.memset(toep[:], 0.0).then_inc(zeroed, 1)

            def readout(o, q):
                c_re = prm[:, bass.ds(PRM["c_re"][0] + o * OGP * C, OGP * C)].rearrange(
                    "p (g c) -> p g c", c=C).unsqueeze(2).to_broadcast([P, OGP, J + 1, C])
                c_im = prm[:, bass.ds(PRM["c_im"][0] + o * OGP * C, OGP * C)].rearrange(
                    "p (g c) -> p g c", c=C).unsqueeze(2).to_broadcast([P, OGP, J + 1, C])

                def lam(table):
                    return table[:, bass.ds(o * OGP, OGP), 0:J + 1].unsqueeze(3).to_broadcast([P, OGP, J + 1, C])

                wait(pool, w_done, 2 * o)
                wait(pool, y_mm, o - 1)
                gate()
                nc.gpsimd.tensor_tensor(w_tmp[:, 0], c_re, lam(l_re), ALU.mult).then_inc(w_step, 1)
                nc.gpsimd.tensor_tensor(w_tmp[:, 1], c_im, lam(nl_im), ALU.mult).then_inc(w_step, 1)
                pool.wait_ge(w_step, 5 * o + 2)
                nc.gpsimd.tensor_tensor(w_ri[:, q, 0], w_tmp[:, 0], w_tmp[:, 1], ALU.add).then_inc(w_step, 1)
                pool.wait_ge(w_step, 5 * o + 3)
                gate()
                nc.gpsimd.tensor_tensor(w_tmp[:, 0], c_re, lam(nl_im), ALU.mult).then_inc(w_step, 1)
                nc.gpsimd.tensor_tensor(w_tmp[:, 1], c_im, lam(nl_re), ALU.mult).then_inc(w_step, 1)
                pool.wait_ge(w_step, 5 * o + 5)
                nc.gpsimd.tensor_tensor(w_ri[:, q, 1], w_tmp[:, 0], w_tmp[:, 1], ALU.add).then_inc(w_done, 1)
                pool.wait_ge(w_done, 2 * o + 1)
                gate()
                r8 = mag[:, bass.ds(o * OGP, OGP), J:J + 1].to_broadcast([P, OGP, NK])
                for ri in range(2):
                    ins = nc.gpsimd.tensor_tensor(decay[:, q, ri], r8,
                                                  C_("keep").unsqueeze(1).to_broadcast([P, OGP, NK]), ALU.mult)
                ins.then_inc(w_done, 1)

            wait(pool, s_cst, 16)
            wait(pool, setup_v, SETUP_POW)
            wait(pool, setup_a, 3)
            readout(0, 0)
            readout(1, 1)
            with pool.Fori(1, NO // 2) as i:
                readout(2 * i, 0)
                readout(2 * i + 1, 1)

            wait(pool, w_done, 2 * NO)
            with pool.Fori(0, NU // 4) as i:
                for s in range(4):
                    pool.wait_ge(raw_in[s % 2], 32 * i + 16 * (s // 2) + 16)
                    gate()
                    nc.gpsimd.tensor_scalar(w_hi[:, s, :], raw[:, s % 2, :], 1.0, 0.0, ALU.mult, ALU.add
                                            ).then_inc(w_hi_done, 1)
                    pool.wait_ge(w_hi_done, 4 * i + s + 1)
                    nc.gpsimd.tensor_tensor(w_lo[:, s, :], raw[:, s % 2, :], w_hi[:, s, :].bitcast(F32),
                                            ALU.subtract).then_inc(w_split, 1)

        @block.scalar
        def _(a):
            act_fn = nc.scalar.activation

            wait(a, s_xu, 16)
            for o in range(NO):
                wait(a, sq_used, o - 1)
                act_fn(y_sb[:, o % 2, :], xy[:, o * OCT:(o + 1) * OCT, :].rearrange("p g k -> p (g k)"),
                       ACT.Square).then_inc(sq_ready, 1)
            wait(a, s_prm, 16)
            act_fn(small[:, 0], PR("log_dt"), ACT.Exp).then_inc(setup_a, 1)
            wait(a, setup_v, SETUP_EXP)
            act_fn(small[:, 4], small[:, 3], ACT.Tanh, scale=0.5).then_inc(setup_a, 1)
            act_fn(mag[:], mag[:], ACT.Exp).then_inc(setup_a, 1)
            wait(a, setup_v, SETUP_PH)
            act_fn(l_im[:], ph[:], ACT.Sin, scale=TWO_PI).then_inc(setup_a, 1)
            act_fn(l_re[:], ph[:], ACT.Sin, scale=PI_).then_inc(setup_a, 1)
            for c in range(4):
                wait(a, setup_v, SETUP_TAB + 5 * c + 3)
                act_fn(sink_[:, 8 * c:8 * c + 8], phk[:], ACT.Sin, scale=TWO_PI).then_inc(setup_a, 1)
                act_fn(cosk[:, 8 * c:8 * c + 8], phk[:], ACT.Sin, scale=PI_).then_inc(setup_a, 1)
            wait(a, setup_v, SETUP_MS)
            act_fn(rstd_u[:, 0], rstd_u[:, 1], ACT.Sqrt).then_inc(setup_a, 1)

            def evacuate(o, q):
                wait(a, t_mm, o + 1)
                act_fn(v_ri[:, q].rearrange("p r g n -> p r (g n)"), ps[:, 0:2, :], ACT.Copy).then_inc(v_evac, 1)
                wait(a, k_mm, o + 1)
                wait(a, t_in[1 - q], 16 * J * ((o + 1) // 2))
                act_fn(k_out[:].rearrange("p e g n -> p e (g n)"), ps[0:C, 2:4, :], ACT.Copy).then_inc(k_evac, 1)

            def gelu(o, q):
                wait(a, y_mm, o + 1)
                wait(a, y_out[1 - q], 16 * J * ((o + 1) // 2))
                act_fn(y_sb[:, q, :].rearrange("p (g e k) -> p e g k", e=2, k=NK),
                       ps[:, 5:7, 0:OGP * NK].rearrange("p e (g k) -> p e g k", k=NK),
                       ACT.Gelu_apprx_tanh).then_inc(gelu_done, 1)

            octets(a, evacuate, gelu)

            for o in range(NO):
                wait(a, y_back[o % 2], 16 * (o // 2 + 1))
                act_fn(hid[:, 0, 0, o, :], xy[:, o * OCT:(o + 1) * OCT, :].rearrange("p g k -> p (g k)"),
                       ACT.Copy).then_inc(y_hi, 1)

            def norm_hi(added, m, outs):
                wait(a, h_added, added)
                for g, dst in outs:
                    act_fn(dst[:, 0, bass.ds(m, 1), :].rearrange("p a n -> p (a n)"),
                           h[:, bass.ds(m, 1), :].rearrange("p a n -> p (a n)"),
                           ACT.Copy, scale=col[:, bass.ds(COL[g][0] + m, 1)]).then_inc(n_hi, 1)

            def root(n):
                wait(a, stat_v, 2 * n + 2)
                act_fn(rstd[:], stat[:], ACT.Sqrt).then_inc(stat_a, 1)

            wait(a, s_h, 16)
            wait(a, s_col, 16)
            with a.Fori(0, KT // 2) as i:
                for e in range(2):
                    a.wait_ge(unit_done, 4 * i + 2 * e + 2)
                    act_fn(t2[:, e, :], ps[:, 2 * e + 1, :], ACT.Sigmoid,
                           bias=col[:, bass.ds(COL["b_gate"][0] + 2 * i + e, 1)]).then_inc(sig_done, 1)
                    norm_hi(2 * i + e + 1, 2 * i + e, [("g_mlp0", act)])

            def mlp(layer):
                n0 = H_MLP[layer]
                root(0 if layer == 0 else 2)

                def hidden(b, par):
                    for m in range(KT):
                        n = NB_FF * KT * layer + KT * b + m
                        a.wait_ge(hid_sq, n + 1)
                        act_fn(hid[:, par, 0, m, :], t2[:, m % 2, :], ACT.Copy).then_inc(hid_hi, 1)

                with a.Fori(0, NB_FF // 2) as i:
                    hidden(2 * i, 0)
                    hidden(2 * i + 1, 1)
                if layer == 0:
                    with a.Fori(0, KT) as m:
                        norm_hi(n0 + (NB_FF - 1) * KT + 1 + m, m, [("g_kv", act), ("g_q", hid[:, 0])])

            mlp(0)
            root(1)
            wait(a, stat_c, 2)
            act_fn(rcol[:], scol[:], ACT.Sqrt).then_inc(stat_a, 1)

            def stage(n, u):
                q = u % 2
                Q = QUADS * n + u
                wait(a, q_done, KT)
                wait(a, pads, 1)
                wait(a, s_mm, Q - 1)
                for e in range(2):
                    r = slice(64 * e, 64 * e + 64)
                    act_fn(qstage[r, q, e:e + 3:2, :], qT[r, 2 * u:2 * u + 2, bass.ds(n * BLK, BLK)],
                           ACT.Copy, scale=HD ** -0.5).then_inc(q_staged, 1)

            def exps(n, u):
                q = u % 2
                Q = QUADS * n + u
                a.wait_ge(m_step, 4 * Q + 4)
                act_fn(es[:, q, :], sm[:, q, :], ACT.Exp).then_inc(es_done, 1)
                for i in range(4):
                    act_fn(s_sb[:, q, i, :], s_sb[:, q, i, :], ACT.Exp, bias=negm[:, q, i:i + 1],
                           accum_out=den[:, q, i:i + 1]).then_inc(p_exp, 1)

            def turned(n, u):
                q = u % 2
                Q = QUADS * n + u
                a.wait_ge(pt_mm, Q + 1)
                act_fn(pT[:, q, 0:2].rearrange("p i b n -> p (i b n)"), ps[:, 4, :], ACT.Copy).then_inc(pt_a, 1)

            def o_hi(n, u):
                q = u % 2
                Q = QUADS * n + u
                a.wait_ge(ot_mm, Q + 1)
                act_fn(hid[:, 0, 0, 2 * u:2 * u + 2, bass.ds(n * BLK, BLK)],
                       ps[:, 7, q * 256:q * 256 + 256].rearrange("p (t n) -> p t n", t=2),
                       ACT.Copy).then_inc(ot_hi, 1)

            skewed(a, [(exps, 0), (stage, -1), (turned, 1), (o_hi, 3)], lambda: stage(0, 0))

            with a.Fori(0, KT) as m:
                norm_hi(H_O + 1 + m, m, [("g_mlp1", act)])
            mlp(1)
            root(3)

        @block.vector
        def _(v):
            tt, ts, stt = nc.vector.tensor_tensor, nc.vector.tensor_scalar, nc.vector.scalar_tensor_tensor
            count = [0]

            def link(ins):
                count[0] += 1
                ins.then_inc(setup_v, 1)
                v.wait_ge(setup_v, count[0])

            def sm_(i):
                return small[:, i]

            def turns(dst, tmp):
                link(ts(tmp, dst, ROUND, ROUND, ALU.add, ALU.subtract))
                link(tt(dst, dst, tmp, ALU.subtract))

            nc.vector.memset(acc[:], 0.0).then_inc(sq_acc, 1)
            nc.vector.memset(stat[:], 0.0).then_inc(bank_free, 4)
            wait(v, s_prm, 16)
            wait(v, s_cst, 16)
            re, im = sm_(1), PR("a_im")
            link(ts(re, PR("a_re"), LAM_MAX, None, ALU.min))
            wait(v, setup_a, 1)
            link(tt(sm_(2), im, sm_(0), ALU.mult))
            link(tt(sm_(3), re, sm_(0), ALU.mult))
            power = C_("pow").unsqueeze(1).to_broadcast([P, GP, NPOW])
            link(tt(mag[:], sm_(3).unsqueeze(2).to_broadcast([P, GP, NPOW]), power, ALU.mult))
            assert count[0] == SETUP_EXP
            link(ts(sm_(2), sm_(2), 1.0 / (2.0 * np.pi), None, ALU.mult))
            turns(sm_(2), sm_(5))
            link(tt(ph[:], sm_(2).unsqueeze(2).to_broadcast([P, GP, NPOW]), power, ALU.mult))
            turns(ph[:], rnd[:])
            assert count[0] == SETUP_PH
            link(ts(sm_(6), sm_(2), float(J), None, ALU.mult))
            turns(sm_(6), sm_(5))
            wait(v, setup_a, 5)
            link(ts(sm_(7), sm_(4), -1.0, 1.0, ALU.mult, ALU.add))
            link(nc.vector.reciprocal(sm_(7), sm_(7)))
            link(stt(sm_(7), sm_(4), 2.0, sm_(7), ALU.mult, ALU.mult))
            sh1 = l_re[:, :, 1:2].rearrange("p g a -> p (g a)")
            link(stt(sm_(8), sh1, -2.0, sh1, ALU.mult, ALU.mult))
            link(stt(sm_(9), sm_(8), 1.0, sm_(7), ALU.add, ALU.mult))
            link(tt(sm_(9), sm_(9), sm_(8), ALU.add))
            link(tt(l_re[:], l_re[:], l_re[:], ALU.mult))
            link(ts(l_re[:], l_re[:], -2.0, 1.0, ALU.mult, ALU.add))
            link(tt(l_re[:], l_re[:], mag[:], ALU.mult))
            link(tt(l_im[:], l_im[:], mag[:], ALU.mult))
            link(ts(nl_re[:], l_re[:, :, 0:J + 1], -1.0, None, ALU.mult))
            link(ts(nl_im[:], l_im[:, :, 0:J + 1], -1.0, None, ALU.mult))
            assert count[0] == SETUP_POW
            li1 = l_im[:, :, 1:2].rearrange("p g a -> p (g a)")
            link(tt(sm_(5), re, re, ALU.mult))
            link(tt(sm_(10), im, im, ALU.mult))
            link(tt(sm_(5), sm_(5), sm_(10), ALU.add))
            link(nc.vector.reciprocal(sm_(5), sm_(5)))
            link(tt(sm_(10), sm_(9), re, ALU.mult))
            link(tt(sm_(11), li1, im, ALU.mult))
            link(tt(sm_(10), sm_(10), sm_(11), ALU.add))
            link(tt(sm_(10), sm_(10), sm_(5), ALU.mult))
            link(tt(sm_(12), li1, re, ALU.mult))
            link(tt(sm_(13), sm_(9), im, ALU.mult))
            link(tt(sm_(12), sm_(12), sm_(13), ALU.subtract))
            link(tt(sm_(12), sm_(12), sm_(5), ALU.mult))
            f_re = sm_(10).unsqueeze(2).to_broadcast([P, GP, J])
            f_im = sm_(12).unsqueeze(2).to_broadcast([P, GP, J])
            lr, li = l_re[:, :, J + 1:], l_im[:, :, J + 1:]
            tmp = rnd[:, :, 0:J]
            link(tt(x_re[:], lr, f_re, ALU.mult))
            link(tt(tmp, li, f_im, ALU.mult))
            link(tt(x_re[:], x_re[:], tmp, ALU.subtract))
            link(tt(x_im[:], lr, f_im, ALU.mult))
            link(tt(tmp, li, f_re, ALU.mult))
            link(tt(x_im[:], x_im[:], tmp, ALU.add))
            assert count[0] == SETUP_TAB
            for c in range(4):
                wait(v, setup_a, 5 + 2 * c)
                link(tt(phk[:], small[:, 6, 8 * c:8 * c + 8].unsqueeze(2).to_broadcast([P, 8, NK]),
                        C_("chunk").unsqueeze(1).to_broadcast([P, 8, NK]), ALU.mult))
                turns(phk[:], phr[:])
                wait(v, setup_a, 7 + 2 * c)
                part = cosk[:, 8 * c:8 * c + 8]
                link(tt(part, part, part, ALU.mult))
                link(ts(part, part, -2.0, 1.0, ALU.mult, ALU.add))
            wait(v, sq_used, NO)
            link(nc.vector.tensor_reduce(rstd_u[:, 0], ps[:, 7, :].rearrange("p (g k) -> p k g", k=NK), AX.X, ALU.add))
            link(ts(rstd_u[:, 0], rstd_u[:, 0], 1.0 / D, EPS, ALU.mult, ALU.add))
            link(nc.vector.reciprocal(rstd_u[:, 1], rstd_u[:, 0]))
            assert count[0] == SETUP_MS
            wait(v, setup_a, 14)
            wait(v, s_dd, 16)

            def project(o, q):
                def b(name):
                    return prm[:, bass.ds(PRM[name][0] + o * OGP * C, OGP * C)].rearrange(
                        "p (g c) -> p g c", c=C).unsqueeze(2).to_broadcast([P, OGP, J, C])

                def x(table):
                    return table[:, bass.ds(o * OGP, OGP), :].unsqueeze(3).to_broadcast([P, OGP, J, C])

                wait(v, y_mm, o - 1)
                wait(v, p_done, o)
                wait(v, u_done, o)
                tt(p_tmp[:, 0], b("b_re"), x(x_re), ALU.mult).then_inc(p_step, 1)
                tt(p_tmp[:, 1], b("b_im"), x(x_im), ALU.mult).then_inc(p_step, 1)
                v.wait_ge(p_step, 5 * o + 2)
                tt(p_ri[:, q, 0], p_tmp[:, 0], p_tmp[:, 1], ALU.subtract).then_inc(p_step, 1)
                v.wait_ge(p_step, 5 * o + 3)
                tt(p_tmp[:, 0], b("b_re"), x(x_im), ALU.mult).then_inc(p_step, 1)
                tt(p_tmp[:, 1], b("b_im"), x(x_re), ALU.mult).then_inc(p_step, 1)
                v.wait_ge(p_step, 5 * o + 5)
                tt(p_ri[:, q, 1], p_tmp[:, 0], p_tmp[:, 1], ALU.add).then_inc(p_done, 1)
                tt(u_tmp[:], xy[:, bass.ds(o * OCT, OCT), :],
                   prm[:, bass.ds(PRM["g_in"][0] + o * OCT, OCT)].unsqueeze(2).to_broadcast([P, OCT, NK]),
                   ALU.mult).then_inc(u_step, 1)
                v.wait_ge(u_step, o + 1)
                tt(u_sb[:, q], u_tmp[:], rstd_u[:, 0].unsqueeze(1).to_broadcast([P, OCT, NK]),
                   ALU.mult).then_inc(u_done, 1)

            def run_states(o, q):
                wait(v, k_evac, o + 1)
                tt(k_out[:, :, :, 0:C], k_out[:, :, :, 0:C],
                   ddiag[:, :, bass.ds(o * OGP, OGP), :], ALU.add).then_inc(k_diag, 1)
                cos = cosk[:, bass.ds(o * OGP, OGP), :].rearrange("p g k -> p (g k)").unsqueeze(1).to_broadcast([P, 2, OGP * NK])
                sin = sink_[:, bass.ds(o * OGP, OGP), :].rearrange("p g k -> p (g k)").unsqueeze(1).to_broadcast([P, 2, OGP * NK])

                def flat(t):
                    return t.rearrange("p r g k -> p r (g k)")

                b = ps[:, 4, :].rearrange("p (r n) -> p r n", r=2)
                wait(v, st_done, 2 * o)
                wait(v, b_mm, o + 1)
                tt(flat(rc[:]), b, cos, ALU.mult).then_inc(rot, 1)
                tt(flat(rs[:]), b, sin, ALU.mult).then_inc(b_read, 1)
                v.wait_ge(rot, 6 * o + 1)
                v.wait_ge(b_read, o + 1)
                tt(rb[:, 0], rc[:, 0], rs[:, 1], ALU.add).then_inc(rot, 1)
                tt(rb[:, 1], rc[:, 1], rs[:, 0], ALU.subtract).then_inc(rot, 1)
                v.wait_ge(rot, 6 * o + 3)
                v.wait_ge(w_done, 2 * o + 2)
                nc.vector.tensor_tensor_scan(rb[:].rearrange("p r g k -> p (r g k)"),
                                             decay[:, q].rearrange("p r g k -> p (r g k)"),
                                             rb[:].rearrange("p r g k -> p (r g k)"),
                                             0.0, ALU.mult, ALU.add).then_inc(rot, 1)
                v.wait_ge(rot, 6 * o + 4)
                tt(flat(rc[:]), flat(rb[:]), cos, ALU.mult).then_inc(rot, 1)
                tt(flat(rs[:]), flat(rb[:]), sin, ALU.mult).then_inc(rot, 1)
                v.wait_ge(rot, 6 * o + 6)
                wait(v, zeroed, 3)
                wait(v, y_mm, o - 1)
                tt(st[:, q, 0, :, 1:], rc[:, 0], rs[:, 1], ALU.subtract).then_inc(st_done, 1)
                tt(st[:, q, 1, :, 1:], rs[:, 0], rc[:, 1], ALU.add).then_inc(st_done, 1)

            octets(v, project, run_states)

            for o in range(NO):
                wait(v, y_hi, o + 1)
                tt(hid[:, 0, 1, o, :], xy[:, o * OCT:(o + 1) * OCT, :].rearrange("p g k -> p (g k)"),
                   hid[:, 0, 0, o, :].bitcast(F32), ALU.subtract).then_inc(y_lo, 1)

            def tile(t, m):
                return t[:, bass.ds(m, 1), :].rearrange("p a n -> p (a n)")

            def normed(added, norm, n_base, m, outs):
                v.wait_ge(h_added, added)
                tt(t1[:], tile(h, m), tile(h, m), ALU.mult).then_inc(sq_tmp, 1)
                v.wait_ge(sq_tmp, norm * KT + m + 1)
                v.wait_ge(sq_acc, norm * (KT + 1) + m + 1)
                tt(acc[:], acc[:], t1[:], ALU.add).then_inc(sq_acc, 1)
                for i, (g, dst) in enumerate(outs):
                    v.wait_ge(n_hi, n_base + i + 1)
                    stt(tile(dst[:, 1], m), tile(h, m), col[:, bass.ds(COL[g][0] + m, 1)],
                        tile(dst[:, 0], m).bitcast(F32), ALU.mult, ALU.subtract).then_inc(n_lo, 1)

            def inverse(n, cols=False):
                wait(v, stat_mm, n + 1)
                if cols:
                    wait(v, stat_col_mm, 1)
                ts(stat[:], ps[:, 7, :], 1.0 / D, EPS, ALU.mult, ALU.add).then_inc(stat_v, 1)
                if cols:
                    ts(scol[:], ps[:, 6, 0:NBLK], 1.0 / D, EPS, ALU.mult, ALU.add).then_inc(stat_c, 1)
                wait(v, stat_v, 2 * n + 1)
                nc.vector.reciprocal(stat[:], stat[:]).then_inc(stat_v, 1)
                nc.vector.memset(acc[:], 0.0).then_inc(sq_acc, 1)
                if cols:
                    v.wait_ge(stat_c, 1)
                    nc.vector.reciprocal(scol[:], scol[:]).then_inc(stat_c, 1)

            wait(v, s_h, 16)
            wait(v, s_col, 16)
            with v.Fori(0, KT // 2) as i:
                for e in range(2):
                    m = 2 * i + e
                    v.wait_ge(sig_done, m + 1)
                    v.wait_ge(sq_acc, m + 1)
                    stt(t1[:], ps[:, 2 * e, :], col[:, bass.ds(COL["b_val"][0] + m, 1)], t2[:, e, :],
                        ALU.add, ALU.mult).then_inc(bank_free, 2)
                    v.wait_ge(bank_free, 4 + 2 * m + 2)
                    hv = tile(h, m).rearrange("p (k j) -> p j k", j=J)
                    tt(hv, t1[:].rearrange("p (j k) -> p j k", j=J), hv, ALU.add).then_inc(h_added, 1)
                    normed(m + 1, 0, m, m, [("g_mlp0", act)])

            def mlp(layer):
                base, n0, norm = U_MLP[layer], H_MLP[layer], 2 * layer
                inverse(norm)
                wait(v, stat_a, STAT_A[norm])

                def hidden(b, par):
                    for m in range(KT):
                        U = base + m + (0 if isinstance(b, int) and b == 0 else 2 * KT * b - KT)
                        n = NB_FF * KT * layer + KT * b + m
                        v.wait_ge(unit_done, U + 1)
                        stt(t1[:], ps[:, m % 4, :], 0.0, rstd[:], ALU.max, ALU.mult).then_inc(bank_free, 1)
                        v.wait_ge(bank_free, 4 + U + 1)
                        tt(t2[:, m % 2, :], t1[:], t1[:], ALU.mult).then_inc(hid_sq, 1)
                        v.wait_ge(hid_hi, n + 1)
                        tt(hid[:, par, 1, m, :], t2[:, m % 2, :], hid[:, par, 0, m, :].bitcast(F32),
                           ALU.subtract).then_inc(hid_lo, 1)

                def output(b, last):
                    U0 = base + 2 * KT * b + (KT if last else 2 * KT)
                    a0 = n0 + KT * b
                    with v.Fori(0, KT // 4) as i:
                        for s in range(4):
                            m = 4 * i + s
                            v.wait_ge(unit_done, U0 + 1 + m)
                            v.wait_ge(h_added, a0 + m)
                            tt(tile(h, m), ps[:, s, :], tile(h, m), ALU.add).then_inc(bank_free, 1)
                            v.wait_ge(bank_free, 4 + U0 + 1 + m)
                            v.sem_inc(h_added, 1)
                            if last and layer == 0:
                                normed(a0 + m + 1, 1, KT + 2 * m, m, [("g_kv", act), ("g_q", hid[:, 0])])
                            elif last:
                                normed(a0 + m + 1, 3, 4 * KT, m, [])

                hidden(0, 0)
                with v.Fori(0, NB_FF // 2 - 1) as i:
                    hidden(2 * i + 1, 1)
                    output(2 * i, False)
                    hidden(2 * i + 2, 0)
                    output(2 * i + 1, False)
                hidden(NB_FF - 1, 1)
                output(NB_FF - 2, False)
                output(NB_FF - 1, True)

            mlp(0)

            inverse(1, cols=True)
            wait(v, stat_a, STAT_A[1])
            nc.vector.memset(kT[:, :, 0:BLK], 0.0).then_inc(pads, 1)
            nc.vector.memset(v_sb[:, 0, :], 0.0).then_inc(pads, 1)
            for t in range(2):
                wait(v, unit_done, U_KV + t + 1)
                wait(v, kv_done, t)
                tt(t1[:], ps[:, t, :], rstd[:], ALU.mult).then_inc(bank_free, 1)
                wait(v, bank_free, 4 + U_KV + t + 1)
                ts(kT[:, t, BLK:], t1[:], COLS("b_k")[:, t:t + 1], None, ALU.add).then_inc(kv_done, 1)
            for t in range(2):
                wait(v, unit_done, U_KV + 2 + t + 1)
                for n in range(NBLK):
                    ins = stt(v_sb[:, 1 + n, t * P:(t + 1) * P], ps[:, 2 + t, n * P:(n + 1) * P], rcol[:, n:n + 1],
                              COLS("b_v")[:, t * P:(t + 1) * P], ALU.mult, ALU.add)
                    ins.then_inc(kv_done, 1)
                v.wait_ge(kv_done, 2 + 4 * (t + 1))
                v.sem_inc(bank_free, 1)
            wait(v, kv_done, 10)
            nc.vector.memset(qstage[:], 0.0).then_inc(pads, 1)
            with v.Fori(0, KT // 4) as i:
                for s in range(4):
                    m = 4 * i + s
                    v.wait_ge(unit_done, U_Q + 1 + m)
                    tt(t1[:], ps[:, s, :], rstd[:], ALU.mult).then_inc(bank_free, 1)
                    v.wait_ge(bank_free, 4 + U_Q + 1 + m)
                    ts(tile(qT, m), t1[:], col[:, bass.ds(COL["b_q"][0] + m, 1)], None, ALU.add).then_inc(q_done, 1)
                    v.wait_ge(q_done, m + 1)
            wait(v, s_mask, 16)

            def maxima(n, u):
                q = u % 2
                Q = QUADS * n + u
                sink = COLS("sink")[:, 4 * u:4 * u + 4]
                v.wait_ge(s_mm, Q + 1)
                tt(s_sb[:, q], ps[:, 2 * q:2 * q + 2, :].rearrange("p a (i n) -> p (a i) n", n=2 * BLK),
                   mask[:, bass.ds(n, 1), :].to_broadcast([P, 4, 2 * BLK]), ALU.add).then_inc(s_masked, 1)
                v.wait_ge(s_masked, Q + 1)
                nc.vector.tensor_reduce(mx[:, q], s_sb[:, q], AX.X, ALU.max).then_inc(m_step, 1)
                v.wait_ge(m_step, 4 * Q + 1)
                tt(mx[:, q], mx[:, q], sink, ALU.max).then_inc(m_step, 1)
                v.wait_ge(m_step, 4 * Q + 2)
                ts(negm[:, q], mx[:, q], -1.0, None, ALU.mult).then_inc(m_step, 1)
                tt(sm[:, q], sink, mx[:, q], ALU.subtract).then_inc(m_step, 1)

            def denominators(n, u):
                q = u % 2
                Q = QUADS * n + u
                v.wait_ge(p_exp, 4 * Q + 4)
                tt(den[:, q], den[:, q], es[:, q], ALU.add).then_inc(den_done, 1)
                v.wait_ge(den_done, Q + 1)
                nc.vector.reciprocal(rden[:, q], den[:, q]).then_inc(rden_done, 1)

            def turned(n, u):
                q = u % 2
                Q = QUADS * n + u
                v.wait_ge(pt_mm, Q + 1)
                ts(pT[:, q, 2:4].rearrange("p i b n -> p (i b n)"), ps[:, 5, :], 1.0, None, ALU.mult).then_inc(pt_v, 1)

            def normalize(n, u):
                q = u % 2
                Q = QUADS * n + u
                v.wait_ge(o_mm, Q + 1)
                v.wait_ge(rden_done, Q + 1)
                tt(o_sb[:, q], ps[:, 6, q * 256:q * 256 + 256].rearrange("p (i d) -> p i d", d=HD),
                   rden[:, q].unsqueeze(2).to_broadcast([P, 4, HD]), ALU.mult).then_inc(o_norm, 1)

            def o_low(n, u):
                q = u % 2
                Q = QUADS * n + u
                v.wait_ge(ot_hi, Q + 1)
                tt(hid[:, 0, 1, 2 * u:2 * u + 2, bass.ds(n * BLK, BLK)],
                   ps[:, 7, q * 256:q * 256 + 256].rearrange("p (t n) -> p t n", t=2),
                   hid[:, 0, 0, 2 * u:2 * u + 2, bass.ds(n * BLK, BLK)].bitcast(F32),
                   ALU.subtract).then_inc(ot_lo, 1)

            skewed(v, [(normalize, 2), (maxima, 0), (turned, 1), (denominators, 0), (o_low, 3)])

            with v.Fori(0, KT // 4) as i:
                for s in range(4):
                    m = 4 * i + s
                    v.wait_ge(unit_done, U_O + 1 + m)
                    stt(tile(h, m), ps[:, s, :], col[:, bass.ds(COL["b_o"][0] + m, 1)], tile(h, m),
                        ALU.add, ALU.add).then_inc(bank_free, 1)
                    v.wait_ge(bank_free, 4 + U_O + 1 + m)
                    v.sem_inc(h_added, 1)
                    normed(H_O + m + 1, 2, 3 * KT + m, m, [("g_mlp1", act)])

            mlp(1)
            inverse(3)
            wait(v, stat_a, STAT_A[3])
            for m in range(KT):
                stt(h[:, m, :], h[:, m, :], COLS("g_out")[:, m:m + 1], rstd[:], ALU.mult, ALU.mult).then_inc(out_t, 1)

        @block.tensor
        def _(pe):
            mm, turn = nc.tensor.matmul, nc.tensor.transpose

            wait(pe, s_cst, 16)
            for o in range(NO):
                wait(pe, sq_ready, o + 1)
                mm(ps[:, 7, :], C_("same_step"), y_sb[:, o % 2, :], start=(o == 0), stop=(o == NO - 1)
                   ).then_inc(sq_used, 1)

            def fold(o, q):
                wait(pe, p_done, o + 1)
                wait(pe, v_evac, o)
                for ri in range(2):
                    for g in range(OGP):
                        last = turn(ps[:, ri, g * P:(g + 1) * P], p_ri[:, q, ri, g].rearrange("p j c -> p (j c)"), ident)
                last.then_inc(t_mm, 1)
                wait(pe, w_done, 2 * o + 2)
                wait(pe, k_evac, o)
                pe.sem_inc(passed, 1)
                for g in range(OGP):
                    for e in range(2):
                        r = slice(64 * e, 64 * e + 64)
                        for ri in range(2):
                            last = mm(ps[0:C, 2 + e, g * P:(g + 1) * P], p_ri[r, q, ri, g, J - 1, :],
                                      w_ri[r, q, ri, g, 0:J, :].rearrange("p j c -> p (j c)"),
                                      start=(ri == 0), stop=(ri == 1))
                last.then_inc(k_mm, 1)
                wait(pe, v_evac, o + 1)
                wait(pe, u_done, o + 1)
                wait(pe, b_read, o)
                for g in range(OGP):
                    for e in range(2):
                        for ri in range(2):
                            last = mm(ps[64 * e:64 * e + 64, 4, (ri * OGP + g) * NK:(ri * OGP + g + 1) * NK],
                                      v_ri[:, q, ri, g, 64 * e:64 * e + 64], u_sb[:, q, 2 * g + e, :],
                                      start=True, stop=True)
                last.then_inc(b_mm, 1)

            def outputs(o, q):
                wait(pe, t_in[q], 16 * J * (o // 2 + 1))
                wait(pe, st_done, 2 * o + 2)
                wait(pe, gelu_done, o)
                for g in range(OGP):
                    for e in range(2):
                        r = slice(64 * e, 64 * e + 64)
                        out = ps[:, 5 + e, g * NK:(g + 1) * NK]
                        mm(out, toep[:, q, e, g, :], u_sb[:, q, 2 * g + e, :], start=True, stop=False)
                        for ri in range(2):
                            last = mm(out, w_ri[r, q, ri, g, 1:J + 1, :].rearrange("p j c -> p (j c)"),
                                      st[r, q, ri, g, 0:NK], start=False, stop=(ri == 1))
                last.then_inc(y_mm, 1)

            octets(pe, fold, outputs)

            def unit(U, s, x, ready=None):
                pe.wait_ge(w_split, U + 1)
                pe.wait_ge(bank_free, U + 1)
                for k in range(KT):
                    if ready is not None:
                        wait(pe, ready[0], ready[1] + ready[2] * k)
                    w = slice(k * P, (k + 1) * P)
                    mm(ps[:, s, :], w_hi[:, s, w], x[:, 0, k, :], start=(k == 0), stop=False)
                    mm(ps[:, s, :], w_hi[:, s, w], x[:, 1, k, :], start=False, stop=False)
                    last = mm(ps[:, s, :], w_lo[:, s, w], x[:, 0, k, :], start=False, stop=(k == KT - 1))
                last.then_inc(unit_done, 1)

            def units(n, U0, x, ready=None):
                with pe.Fori(0, n // 4) as i:
                    for s in range(4):
                        unit(U0 + 4 * i + s, s, x, ready)

            def stats(norm):
                wait(pe, sq_acc, (norm + 1) * (KT + 1))
                mm(ps[:, 7, :], ones, acc[:], start=True, stop=True).then_inc(stat_mm, 1)

            def mlp(layer):
                base = U_MLP[layer]
                n_lo0 = 0 if layer == 0 else 3 * KT
                for s in range(4):
                    unit(base + s, s, act, (n_lo, n_lo0 + 1, 1))
                    if s == 0:
                        stats(2 * layer)
                units(4, base + 4, act)

                def second(b, U0, par):
                    pe.wait_ge(hid_lo, NB_FF * KT * layer + KT * b + KT)
                    units(KT, U0, hid[:, par])

                with pe.Fori(0, NB_FF // 2 - 1) as i:
                    units(KT, base + KT + 4 * KT * i, act)
                    second(2 * i, base + 2 * KT + 4 * KT * i, 0)
                    units(KT, base + 3 * KT + 4 * KT * i, act)
                    second(2 * i + 1, base + 4 * KT + 4 * KT * i, 1)
                units(KT, base + (2 * NB_FF - 3) * KT, act)
                second(NB_FF - 2, base + (2 * NB_FF - 2) * KT, 0)
                second(NB_FF - 1, base + (2 * NB_FF - 1) * KT, 1)

            units(2 * KT, U_GLU, hid[:, 0], (y_lo, 1, 1))
            mlp(0)

            for t in range(2):
                unit(U_KV + t, t, act, (n_lo, KT + 1, 2))
                if t == 0:
                    stats(1)
                    for n in range(NBLK):
                        last = mm(ps[:, 6, n:n + 1], acc[:, n * P:(n + 1) * P], ones[:, 0:1], start=True, stop=True)
                    last.then_inc(stat_col_mm, 1)
            for t in range(2):
                s = 2 + t
                wait(pe, w_split, U_KV + s + 1)
                wait(pe, bank_free, U_KV + s + 1)
                for n in range(NBLK):
                    tok = slice(n * P, (n + 1) * P)
                    for k in range(KT):
                        w = slice(k * P, (k + 1) * P)
                        mm(ps[:, s, tok], act[:, 0, k, tok], w_hi[:, s, w], start=(k == 0), stop=False)
                        mm(ps[:, s, tok], act[:, 0, k, tok], w_lo[:, s, w], start=False, stop=False)
                        last = mm(ps[:, s, tok], act[:, 1, k, tok], w_hi[:, s, w], start=False, stop=(k == KT - 1))
                last.then_inc(unit_done, 1)
            units(KT, U_Q, hid[:, 0], (n_lo, KT + 2, 2))

            def scores(n, u):
                q = u % 2
                Q = QUADS * n + u
                wait(pe, q_staged, 2 * Q + 2)
                wait(pe, s_masked, Q - 1)
                wait(pe, kv_done, 10)
                wait(pe, pads, 3)
                if isinstance(n, int) and Q < 2:
                    wait(pe, bank_free, 4 + U_O)
                for i in range(4):
                    last = mm(ps[:, 2 * q + i // 2, (i % 2) * 2 * BLK:(i % 2 + 1) * 2 * BLK], qstage[:, q, i, :],
                              kT[:, u // 2, bass.ds(n * BLK, 2 * BLK)], start=True, stop=True)
                last.then_inc(s_mm, 1)

            def turn_p(n, u):
                q = u % 2
                Q = QUADS * n + u
                pe.wait_ge(p_exp, 4 * Q + 4)
                wait(pe, pt_a, Q)
                wait(pe, pt_v, Q)
                for i in range(4):
                    for b in range(2):
                        at = (i % 2) * 2 * BLK + b * BLK
                        last = turn(ps[:, 4 + i // 2, at:at + BLK], s_sb[:, q, i, b * BLK:(b + 1) * BLK], ident)
                last.then_inc(pt_mm, 1)

            def mix(n, u):
                q = u % 2
                Q = QUADS * n + u
                pe.wait_ge(pt_a, Q + 1)
                pe.wait_ge(pt_v, Q + 1)
                wait(pe, o_norm, Q)
                for i in range(4):
                    kvh = 2 * (u // 2) + i % 2
                    for b in range(2):
                        last = mm(ps[:, 6, q * 256 + i * HD:q * 256 + (i + 1) * HD], pT[:, q, i, b, :],
                                  v_sb[:, bass.ds(n + b, 1), kvh * HD:(kvh + 1) * HD].rearrange("p a d -> p (a d)"),
                                  start=(b == 0), stop=(b == 1))
                last.then_inc(o_mm, 1)

            def turn_o(n, u):
                q = u % 2
                Q = QUADS * n + u
                pe.wait_ge(o_norm, Q + 1)
                wait(pe, ot_lo, Q)
                for t in range(2):
                    last = turn(ps[:, 7, q * 256 + t * P:q * 256 + (t + 1) * P],
                                o_sb[:, q, 2 * t:2 * t + 2, :].rearrange("p e d -> p (e d)"), ident)
                last.then_inc(ot_mm, 1)

            skewed(pe, [(scores, 0), (turn_p, 1), (mix, 2), (turn_o, 3)])

            pe.wait_ge(ot_lo, QUADS * NBLK)
            units(KT, U_O, hid[:, 0])
            mlp(1)
            stats(3)


def skewed(eng, stages, before=None):
    last = QUADS * NBLK
    longest = max(lag for _, lag in stages)
    if before:
        before()
    for Q in range(QUADS):
        for stage, lag in stages:
            if Q - lag >= 0:
                stage((Q - lag) // QUADS, (Q - lag) % QUADS)
    with eng.Fori(1, NBLK - 1) as n:
        for u in range(QUADS):
            for stage, lag in stages:
                stage(n + (u - lag) // QUADS, (u - lag) % QUADS)
    for Q in range(last - QUADS, last + longest):
        for stage, lag in stages:
            if Q - lag < last:
                stage((Q - lag) // QUADS, (Q - lag) % QUADS)


def _feature_rows(a):
    return a.T.reshape(KT, P, L).transpose(1, 0, 2)


def _panels(w):
    n = w.shape[1] // P
    return w.reshape(KT, P, n, P).transpose(2, 1, 0, 3).reshape(n, P, KT * P)


def kernel(**inputs):
    from concourse import bacc
    from concourse.bass_utils import run_bass_kernel_spmd

    f = {k: np.asarray(v) for k, v in inputs.items()}
    x = f["x"][0]

    def states(a):
        a = a.reshape((GP, 2, S) + a.shape[2:])
        return np.moveaxis(a, 0, 2).reshape((P, GP) + a.shape[3:])

    def cols(a):
        return a.reshape(-1, P).T

    def rows(a):
        return np.broadcast_to(a, (P, a.size))

    group = NQ // NKV
    heads = [(2 * (t // group) + e) * group + t % group for t in range(NQ // 2) for e in range(2)]

    panels = []
    glu = _panels(f["s5_w_glu"][0])
    for m in range(KT):
        panels += [glu[m], glu[KT + m]]

    def mlp(layer):
        w_in = _panels(f["w_mlp_in"][layer])
        w_out = [_panels(f["w_mlp_out"][layer][b * D:(b + 1) * D]) for b in range(NB_FF)]
        order = [w_in[0:KT]]
        for b in range(1, NB_FF):
            order += [w_in[b * KT:(b + 1) * KT], w_out[b - 1]]
        order.append(w_out[NB_FF - 1])
        return [p for block in order for p in block]

    panels += mlp(0)
    panels += list(_panels(f["w_kv"]))
    panels += list(_panels(f["w_q"][0].reshape(D, NQ, HD)[:, heads].reshape(D, D)))
    panels += list(_panels(f["w_o"][0].reshape(NQ, HD, D)[heads].reshape(D, D)))
    panels += mlp(1)

    g_in = np.broadcast_to(f["norm_mix"][0].reshape(G, C).T[None], (J, C, G)).reshape(P, G)
    prm = np.concatenate([
        states(f["s5_a_re"][0]), states(f["s5_a_im"][0]),
        states(np.broadcast_to(f["s5_log_dt"][0][:, None], (G, S))),
        states(f["s5_b_re"][0]).reshape(P, -1), states(f["s5_b_im"][0]).reshape(P, -1),
        states(f["s5_c_re"][0].transpose(0, 2, 1)).reshape(P, -1),
        states(f["s5_c_im"][0].transpose(0, 2, 1)).reshape(P, -1), g_in], axis=1)
    skip = f["s5_d"][0].reshape(GP, 2, C)
    ddiag = np.zeros((C, 2, GP, C), np.float32)
    for c in range(C):
        ddiag[c, :, :, c] = skip[:, :, c].T
    b_kv, b_glu = f["b_kv"], f["s5_b_glu"][0]
    col = np.concatenate([
        cols(b_glu[:D]), cols(b_glu[D:]), cols(f["norm_mlp"][0]), cols(f["norm_kv"]), cols(f["norm_mix"][1]),
        cols(f["norm_mlp"][1]), cols(f["norm_final"]), cols(b_kv[:NKV * HD]),
        cols(f["b_q"][0].reshape(NQ, HD)[heads].reshape(-1)), cols(f["b_o"][0]), rows(b_kv[NKV * HD:]),
        rows(f["sinks"][0][heads])], axis=1)

    keep = np.ones(NK)
    keep[0] = 0
    step = np.arange(P) // C
    cst = np.concatenate([
        rows(np.concatenate([np.arange(J + 1), np.arange(J)[::-1]])), rows(np.arange(NK)), rows(keep),
        step[:, None] == step[None, :], np.eye(P), np.ones((P, P))], axis=1).astype(np.float32)
    back = np.arange(BLK)[:, None] + BLK - np.arange(2 * BLK)[None, :]
    inside = (back >= 0) & (back < BLK)
    first = inside & (np.arange(2 * BLK) >= BLK)[None, :]
    mask = np.where(np.stack([first] + [inside] * (NBLK - 1), axis=1), 0.0, -1e30).astype(np.float32)

    arrays = {
        "panels": np.stack(panels),
        "xu": x.reshape(NK, J, G, C).transpose(1, 3, 2, 0).reshape(P, G, NK),
        "x_rows": _feature_rows(x), "prm": prm, "ddiag": ddiag, "cst": cst, "mask": mask, "col": col,
    }
    arrays = {k + "_in": np.ascontiguousarray(v) for k, v in arrays.items()}
    nc = bacc.Bacc("TRN2", target_bir_lowering=False, num_devices=1)
    aps = [nc.dram_tensor(k, v.shape, F32, kind="ExternalInput").ap() for k, v in arrays.items()]
    out = nc.dram_tensor("out", (KT, P, L), F32, kind="ExternalOutput").ap()
    build(nc, *aps, out)
    r = run_bass_kernel_spmd(nc, [arrays], core_ids=[0])
    return r.results[0]["out"].transpose(2, 0, 1).reshape(1, L, D)
```

```python
from contextlib import ExitStack

import numpy as np

import concourse.bass as bass
from concourse import mybir

F32 = mybir.dt.float32
F32R = mybir.dt.float32r
ALU = mybir.AluOpType
ACT = mybir.ActivationFunctionType
AX = mybir.AxisListType

P = 128
D = 1024
L = 512
KT = D // P
FF = 4 * D
NB_FF = FF // D
EPS = 1e-5
J = 8
NK = L // J
C = 16
G = D // C
S = 64
GP = G // 2
OCT = 8
NO = G // OCT
OGP = OCT // 2
HD = 64
NQ = 16
NKV = 4
BLK = 128
NBLK = L // BLK
QUADS = 4
LAM_MAX = -1e-4

U_GLU = 0
U_MLP = (U_GLU + 2 * KT, U_GLU + 2 * KT + 2 * NB_FF * KT + 4 + 2 * KT)
U_KV = U_MLP[0] + 2 * NB_FF * KT
U_Q = U_KV + 4
U_O = U_Q + KT
NU = U_MLP[1] + 2 * NB_FF * KT
assert U_O + KT == U_MLP[1] and U_GLU == 0

PRM = {}
_at = 0
for _name, _n in (("a_re", GP), ("a_im", GP), ("log_dt", GP), ("b_re", GP * C), ("b_im", GP * C),
                  ("c_re", GP * C), ("c_im", GP * C), ("g_in", G)):
    PRM[_name] = (_at, _at + _n)
    _at += _n
N_PRM = _at
N_LAM = PRM["log_dt"][1]
NPOW = (J + 1) + J
CST = {}
_at = 0
for _name, _n in (("pow", NPOW), ("chunk", NK), ("keep", NK), ("same_step", P), ("ident", P), ("ones", P)):
    CST[_name] = (_at, _at + _n)
    _at += _n
N_CST = _at
COL = {}
_at = 0
for _name, _n in (("b_val", KT), ("b_gate", KT), ("g_mlp0", KT), ("g_kv", KT), ("g_q", KT), ("g_mlp1", KT),
                  ("g_out", KT), ("b_k", 2), ("b_q", KT), ("b_o", KT), ("b_v", NKV * HD), ("sink", NQ)):
    COL[_name] = (_at, _at + _n)
    _at += _n
N_COL = _at

H_MLP = (KT, KT + NB_FF * KT + KT)
H_O = KT + NB_FF * KT
SETUP_EXP, SETUP_PH, SETUP_POW, SETUP_MS = 4, 10, 25, 46
STAT_A = (1, 3, 4, 5)

TWO_PI = 6.283185
PI_ = 3.1415925
ROUND = 1.5 * 2.0 ** 23


def build(nc, panels, xu_d, x_d, prm_d, ddiag_d, cst_d, mask_d, col_d, out_d):
    ctx = ExitStack()
    with ctx:
        def sb(name, shape, dt=F32, where=ctx):
            return where.enter_context(nc.sbuf_tensor(name, shape, dt))

        def sem(name):
            return ctx.enter_context(nc.semaphore(name))

        h = sb("h", [P, KT, L])
        raw = sb("raw", [P, 2, D])
        early = ExitStack()
        w_tmp = sb("w_tmp", [P, 4, OGP, J + 1, C], where=early)
        p_tmp = sb("p_tmp", [P, 4, OGP, J, C], where=early)
        early.close()
        w_hi = sb("w_hi", [P, 4, D], F32R)
        w_lo = sb("w_lo", [P, 4, D], F32R)
        cst = sb("cst", [P, N_CST])
        col = sb("col", [P, N_COL])
        acc = sb("acc", [P, L])
        rstd = sb("rstd", [P, L])
        rcol = sb("rcol", [P, NBLK])
        stat = sb("stat", [P, L])
        scol = sb("scol", [P, NBLK])
        gate_sb = sb("gate_sb", [P, 2])
        t1 = sb("t1", [P, L])
        t2 = sb("t2", [P, 2, L])

        s5 = ExitStack()
        prm = sb("prm", [P, N_PRM], where=s5)
        ddiag = sb("ddiag", [C, 2, GP, C], where=s5)
        small = sb("small", [P, 16, GP], where=s5)
        ph = sb("ph", [P, GP, NPOW], where=s5)
        mag = sb("mag", [P, GP, NPOW], where=s5)
        rnd = sb("rnd", [P, GP, NPOW], where=s5)
        l_im = sb("l_im", [P, GP, NPOW], where=s5)
        l_re = sb("l_re", [P, GP, NPOW], where=s5)
        nl_re = sb("nl_re", [P, GP, J + 1], where=s5)
        nl_im = sb("nl_im", [P, GP, J + 1], where=s5)
        x_re = sb("x_re", [P, GP, J], where=s5)
        x_im = sb("x_im", [P, GP, J], where=s5)
        cosk = sb("cosk", [P, GP, NK], where=s5)
        sink_ = sb("sink_", [P, GP, NK], where=s5)
        phk = t1.rearrange("p (g k) -> p g k", k=NK)
        phr = rstd.rearrange("p (g k) -> p g k", k=NK)
        rstd_u = sb("rstd_u", [P, 2, NK], where=s5)
        p_ri = sb("p_ri", [P, 2, 2, OGP, J, C], where=s5)
        u_sb = sb("u_sb", [P, 2, OCT, NK], where=s5)
        w_k = sb("w_k", [P, 2, OGP, J + 1, C], where=s5)
        w_ri = sb("w_ri", [P, 2, 2, OGP, J + 1, C], where=s5)
        v_ri = sb("v_ri", [P, 2, 2, OGP, P], where=s5)
        k_out = sb("k_out", [C, 2, OGP, P], where=s5)
        toep = sb("toep", [P, 2, 2, OGP, P], where=s5)
        decay = sb("decay", [P, 2, 2, OGP, NK], where=s5)
        rc = sb("rc", [P, 2, OGP, NK], where=s5)
        rs = sb("rs", [P, 2, OGP, NK], where=s5)
        rb = sb("rb", [P, 2, OGP, NK], where=s5)
        st = sb("st", [P, 2, 2, OGP, NK + 1], where=s5)
        y_sb = sb("y_sb", [P, 2, OCT * NK], where=s5)
        xy = sb("xy", [P, G, NK], where=s5)
        s5.close()

        hid = sb("hid", [P, 2, 2, KT, L], F32R)
        over = ExitStack()
        act = sb("act", [P, 2, KT, L], F32R, where=over)
        over.close()
        over = ExitStack()
        qT = sb("qT", [P, KT, L], where=over)
        qstage = sb("qstage", [P, 2, 4, BLK], where=over)
        pT = sb("pT", [P, 2, 4, 2, BLK], where=over)
        o_sb = sb("o_sb", [P, 2, 4, HD], where=over)
        fill = sb("fill", [P, 32 * 256 - (KT * L + 2 * 4 * BLK + 2 * 4 * 2 * BLK + 2 * 4 * HD)], where=over)
        kT = sb("kT", [P, 2, BLK + L], where=over)
        v_sb = sb("v_sb", [P, 1 + NBLK, NKV * HD], where=over)
        s_sb = sb("s_sb", [P, 2, 4, 2 * BLK], where=over)
        mask = sb("mask", [P, NBLK, 2 * BLK], where=over)
        mx = sb("mx", [P, 2, 4], where=over)
        negm = sb("negm", [P, 2, 4], where=over)
        sm = sb("sm", [P, 2, 4], where=over)
        es = sb("es", [P, 2, 4], where=over)
        den = sb("den", [P, 2, 4], where=over)
        rden = sb("rden", [P, 2, 4], where=over)
        over.close()

        ps = ctx.enter_context(nc.psum_tensor("ps", [P, 8, 512], F32))

        s_lam, s_prm, s_cst, s_h, s_col, s_mask, s_dd = (sem(n) for n in (
            "lam_in", "prm_in", "cst_in", "h_in", "col_in", "mask_in", "ddiag_in"))
        s_xu = [sem(f"xu_in{c}") for c in range(4)]
        raw_in = [sem("raw_in0"), sem("raw_in1")]
        w_hi_done, w_split = sem("w_hi_done"), sem("w_split")
        unit_done, bank_free = sem("unit_done"), sem("bank_free")
        setup_v, setup_a = sem("setup_v"), sem("setup_a")
        frame_v, frame_a = sem("frame_v"), sem("frame_a")
        sq_ready, sq_used = sem("sq_ready"), sem("sq_used")
        zeroed, passed = sem("zeroed"), sem("passed")
        p_step, p_done, w_copied = sem("p_step"), sem("p_done"), sem("w_copied")
        u_step, u_done, u_copied = sem("u_step"), sem("u_done"), sem("u_copied")
        w_step, w_done = sem("w_step"), sem("w_done")
        t_mm, k_mm, b_mm, y_mm = sem("t_mm"), sem("k_mm"), sem("b_mm"), sem("y_mm")
        v_evac, k_evac, k_diag = sem("v_evac"), sem("k_evac"), sem("k_diag")
        b_read, rot, st_done = sem("b_read"), sem("rot"), sem("st_done")
        t_in = [sem("toep_in0"), sem("toep_in1")]
        gelu_done = sem("gelu_done")
        y_evac, y_turned = sem("y_evac"), sem("y_turned")
        y_hi, y_lo = sem("y_hi"), sem("y_lo")
        sig_done, glu_val = sem("sig_done"), sem("glu_val")
        h_added, sq_tmp, sq_acc = sem("h_added"), sem("sq_tmp"), sem("sq_acc")
        n_hi, n_lo = sem("n_hi"), sem("n_lo")
        stat_mm, stat_v, stat_a = sem("stat_mm"), sem("stat_v"), sem("stat_a")
        stat_col_mm, stat_c = sem("stat_col_mm"), sem("stat_c")
        hid_t, hid_sq, hid_hi, hid_lo = sem("hid_t"), sem("hid_sq"), sem("hid_hi"), sem("hid_lo")
        kv_tmp, kv_done, pads = sem("kv_tmp"), sem("kv_done"), sem("pads")
        q_tmp, q_done = sem("q_tmp"), sem("q_done")
        q_staged, s_mm, s_masked, m_step = sem("q_staged"), sem("s_mm"), sem("s_masked"), sem("m_step")
        p_exp, es_done, den_done, rden_done = sem("p_exp"), sem("es_done"), sem("den_done"), sem("rden_done")
        pt_mm, pt_v, pt_a = sem("pt_mm"), sem("pt_v"), sem("pt_a")
        o_mm, o_norm, ot_mm, ot_hi, ot_lo = sem("o_mm"), sem("o_norm"), sem("ot_mm"), sem("ot_hi"), sem("ot_lo")
        out_t, out_s = sem("out_tile"), sem("out_stored")

        def wait(eng, s, value):
            if not (isinstance(value, int) and value <= 0):
                eng.wait_ge(s, value)

        def C_(name):
            a, b = CST[name]
            return cst[:, a:b]

        def COLS(name):
            a, b = COL[name]
            return col[:, a:b]

        def PR(name):
            a, b = PRM[name]
            return prm[:, a:b]

        def octets(eng, stages, frame=None, frame_end=None, late=None):
            if frame:
                frame(0)
            if frame_end:
                frame_end(0)
            for o in range(-2, 2):
                for stage, lag in stages:
                    if 0 <= o - lag:
                        stage(o - lag, (o - lag) % 2)
                if frame and o == -1:
                    frame(1)
                if frame_end and o == -1:
                    frame_end(1)
            with eng.Fori(1, NO // 2 - 1) as i:
                if frame:
                    frame(i + 1)
                for s in range(2):
                    for stage, lag in stages:
                        stage(2 * i + (s - lag), (s - lag) % 2)
                if frame_end:
                    frame_end(i + 1)
            for o in range(NO - 2, NO + 2):
                if o == NO and late:
                    late()
                for stage, lag in stages:
                    if o - lag < NO:
                        stage(o - lag, (o - lag) % 2)

        def swapped_first(ahead, here):
            def ahead_(o, q):
                if not (isinstance(o, int) and o == 1):
                    ahead(o, q)

            def here_(o, q):
                here(o, q)
                if isinstance(o, int) and o == 0:
                    ahead(1, 1)

            return [(ahead_, -1), (here_, 0)]

        ident, ones = C_("ident"), C_("ones")
        block = ctx.enter_context(nc.Block())

        @block.sync
        def _(sp):
            sp.dma_start(prm[:, 0:N_LAM], prm_d[:, 0:N_LAM]).then_inc(s_lam, 16)
            sp.dma_start(cst[:], cst_d).then_inc(s_cst, 16)
            for c in range(4):
                part = slice(2 * c * OCT, (2 * c + 2) * OCT)
                sp.dma_start(xy[:, part, :], xu_d[:, part, :]).then_inc(s_xu[c], 16)
            sp.dma_start(prm[:, N_LAM:], prm_d[:, N_LAM:]).then_inc(s_prm, 16)
            sp.dma_start(ddiag[:], ddiag_d).then_inc(s_dd, 16)
            sp.dma_start(col[:], col_d).then_inc(s_col, 16)
            for s in range(2):
                sp.dma_start(raw[:, s, :], panels[s]).then_inc(raw_in[s], 16)
            sp.dma_start(h[:], x_d).then_inc(s_h, 16)

            def toeplitz(o, q):
                wait(sp, k_diag, o + 1)
                wait(sp, zeroed, 3)
                for j in range(J):
                    sp.dma_start(toep[j * C:(j + 1) * C, q, :, :, j * C:].rearrange("p e g n -> p (e g) n"),
                                 k_out[:, :, :, 0:(J - j) * C].rearrange("p e g n -> p (e g) n")
                                 ).then_inc(t_in[q], 16)

            def next_panels():
                for u in (2, 3):
                    wait(sp, w_split, u - 1)
                    sp.dma_start(raw[:, u % 2, :], panels[u]).then_inc(raw_in[u % 2], 16)

            octets(sp, [(toeplitz, 0)], late=next_panels)


            wait(sp, y_lo, KT)
            sp.dma_start(mask[:], mask_d).then_inc(s_mask, 16)
            with sp.Fori(2, NU // 2) as i:
                for s in range(2):
                    sp.wait_ge(w_split, 2 * i + s - 1)
                    sp.sem_inc(passed, 1)
                    sp.wait_ge(unit_done, 2 * i + s - 3)
                    sp.sem_inc(passed, 1)
                    sp.dma_start(raw[:, s, :], panels[2 * i + s]).then_inc(raw_in[s], 16)
            for m in range(KT):
                wait(sp, out_t, m + 1)
                sp.dma_start(out_d[m], h[:, m, :]).then_inc(out_s, 16)
            sp.wait_ge(out_s, 16 * KT)

        @block.gpsimd
        def _(pool):
            def gate():
                nc.gpsimd.tensor_tensor(gate_sb[:, 0:1], gate_sb[:, 1:2], gate_sb[:, 1:2], ALU.mult)

            nc.gpsimd.memset(gate_sb[:], 0.0).then_inc(zeroed, 1)
            wait(pool, zeroed, 1)

            nc.gpsimd.memset(st[:], 0.0).then_inc(zeroed, 1)
            nc.gpsimd.memset(toep[:], 0.0).then_inc(zeroed, 1)

            def readout(o, q):
                c_re = prm[:, bass.ds(PRM["c_re"][0] + o * OGP * C, OGP * C)].rearrange(
                    "p (g c) -> p g c", c=C).unsqueeze(2).to_broadcast([P, OGP, J + 1, C])
                c_im = prm[:, bass.ds(PRM["c_im"][0] + o * OGP * C, OGP * C)].rearrange(
                    "p (g c) -> p g c", c=C).unsqueeze(2).to_broadcast([P, OGP, J + 1, C])

                def lam(table):
                    return table[:, bass.ds(o * OGP, OGP), 0:J + 1].unsqueeze(3).to_broadcast([P, OGP, J + 1, C])

                wait(pool, w_done, 2 * o)
                gate()
                for i, (c, table) in enumerate(((c_re, l_re), (c_im, nl_im), (c_re, nl_im), (c_im, nl_re))):
                    nc.gpsimd.tensor_tensor(w_tmp[:, i], c, lam(table), ALU.mult).then_inc(w_step, 1)
                pool.wait_ge(w_step, 4 * o + 4)
                wait(pool, k_mm, o)
                wait(pool, w_copied, o)
                wait(pool, st_done, 2 * o - 2)
                gate()
                nc.gpsimd.tensor_tensor(w_k[:], w_tmp[:, 0:3:2], w_tmp[:, 1:4:2], ALU.add).then_inc(w_done, 1)
                r8 = mag[:, bass.ds(o * OGP, OGP), J:J + 1].to_broadcast([P, OGP, NK])
                for ri in range(2):
                    ins = nc.gpsimd.tensor_tensor(decay[:, q, ri], r8,
                                                  C_("keep").unsqueeze(1).to_broadcast([P, OGP, NK]), ALU.mult)
                ins.then_inc(w_done, 1)

            wait(pool, s_cst, 16)
            wait(pool, s_prm, 16)
            wait(pool, setup_v, SETUP_POW)
            wait(pool, setup_a, 3)
            readout(0, 0)
            wait(pool, sq_ready, NO)
            for o in range(NO):
                part = xy[:, o * OCT:(o + 1) * OCT, :]
                nc.gpsimd.tensor_tensor(part, part, PR("g_in")[:, o * OCT:(o + 1) * OCT].unsqueeze(2).to_broadcast(
                    [P, OCT, NK]), ALU.mult).then_inc(u_step, 1)
            readout(1, 1)
            with pool.Fori(1, NO // 2) as i:
                readout(2 * i, 0)
                readout(2 * i + 1, 1)

            wait(pool, w_done, 2 * NO)
            wait(pool, p_done, 2 * NO)
            with pool.Fori(0, NU // 4) as i:
                for s in range(4):
                    pool.wait_ge(raw_in[s % 2], 32 * i + 16 * (s // 2) + 16)
                    gate()
                    nc.gpsimd.tensor_scalar(w_hi[:, s, :], raw[:, s % 2, :], 1.0, 0.0, ALU.mult, ALU.add
                                            ).then_inc(w_hi_done, 1)
                    pool.wait_ge(w_hi_done, 4 * i + s + 1)
                    nc.gpsimd.tensor_tensor(w_lo[:, s, :], raw[:, s % 2, :], w_hi[:, s, :].bitcast(F32),
                                            ALU.subtract).then_inc(w_split, 1)

        @block.scalar
        def _(a):
            act_fn = nc.scalar.activation

            wait(a, s_lam, 16)
            act_fn(small[:, 0], PR("log_dt"), ACT.Exp).then_inc(setup_a, 1)
            wait(a, setup_v, SETUP_EXP)
            act_fn(small[:, 4], small[:, 3], ACT.Tanh, scale=0.5).then_inc(setup_a, 1)
            act_fn(mag[:], mag[:], ACT.Exp).then_inc(setup_a, 1)
            wait(a, setup_v, SETUP_PH)
            act_fn(l_im[:], ph[:], ACT.Sin, scale=TWO_PI).then_inc(setup_a, 1)
            act_fn(l_re[:], ph[:], ACT.Sin, scale=PI_).then_inc(setup_a, 1)
            for o in range(NO):
                wait(a, s_xu[o // 2], 16)
                wait(a, sq_used, o - 1)
                act_fn(y_sb[:, o % 2, :], xy[:, o * OCT:(o + 1) * OCT, :].rearrange("p g k -> p (g k)"),
                       ACT.Square).then_inc(sq_ready, 1)

            wait(a, setup_v, SETUP_MS)
            act_fn(rstd_u[:, 0], rstd_u[:, 1], ACT.Sqrt).then_inc(setup_a, 1)

            def frame(c):
                wait(a, frame_v, 5 * c + 3)
                pairs = bass.ds(8 * c, 8)
                act_fn(sink_[:, pairs], phk[:], ACT.Sin, scale=TWO_PI).then_inc(frame_a, 1)
                act_fn(cosk[:, pairs], phk[:], ACT.Sin, scale=PI_).then_inc(frame_a, 1)

            def copy_u(o, q):
                wait(a, u_done, o + 1)
                wait(a, y_mm, o - 1)
                act_fn(u_sb[:, q].rearrange("p g k -> p (g k)"),
                       xy[:, bass.ds(o * OCT, OCT), :].rearrange("p g k -> p (g k)"), ACT.Copy).then_inc(u_copied, 1)

            def copy_w(o, q):
                wait(a, w_done, 2 * o + 1)
                wait(a, y_mm, o - 1)
                act_fn(w_ri[:, q].rearrange("p r g j c -> p (r g j c)"),
                       w_k[:].rearrange("p r g j c -> p (r g j c)"), ACT.Copy).then_inc(w_copied, 1)

            def evacuate_v(o, q):
                wait(a, t_mm, o + 1)
                act_fn(v_ri[:, q].rearrange("p r g n -> p r (g n)"), ps[:, 0:2, :], ACT.Copy).then_inc(v_evac, 1)

            def evacuate_k(o, q):
                wait(a, k_mm, o + 1)
                wait(a, t_in[1 - q], 16 * J * ((o + 1) // 2))
                act_fn(k_out[:].rearrange("p e g n -> p e (g n)"), ps[0:C, 2:4, :], ACT.Copy).then_inc(k_evac, 1)

            y_rows = y_sb[0:NK].rearrange("p a n -> p (a n)")

            def evacuate_y(o, q):
                wait(a, y_mm, o + 1)
                wait(a, y_turned, o)
                for e in range(2):
                    act_fn(y_rows.rearrange("p (j g e c) -> p e g j c", j=J, g=OGP, e=2)[:, e],
                           ps[0:NK, 5 + e, :].rearrange("p (g j c) -> p g j c", j=J, c=C), ACT.Copy).then_inc(y_evac, 1)

            def gelu(o, q):
                wait(a, y_turned, o + 1)
                act_fn(xy[:, bass.ds(o * OCT, OCT), :].rearrange("p g k -> p (g k)"), ps[:, 7, :],
                       ACT.Gelu_apprx_tanh).then_inc(gelu_done, 1)

            ahead, here = swapped_first(evacuate_v, evacuate_k)
            octets(a, [(copy_u, 0), (evacuate_y, 2), ahead, (copy_w, 0), here, (gelu, 2)], frame)

            for o in range(NO):
                wait(a, gelu_done, o + 1)
                act_fn(hid[:, 0, 0, o, :], xy[:, o * OCT:(o + 1) * OCT, :].rearrange("p g k -> p (g k)"),
                       ACT.Copy).then_inc(y_hi, 1)

            def norm_hi(added, m, outs):
                wait(a, h_added, added)
                for g, dst in outs:
                    act_fn(dst[:, 0, bass.ds(m, 1), :].rearrange("p a n -> p (a n)"),
                           h[:, bass.ds(m, 1), :].rearrange("p a n -> p (a n)"),
                           ACT.Copy, scale=col[:, bass.ds(COL[g][0] + m, 1)]).then_inc(n_hi, 1)

            def root(n):
                wait(a, stat_v, 2 * n + 2)
                act_fn(rstd[:], stat[:], ACT.Sqrt).then_inc(stat_a, 1)

            wait(a, s_h, 16)
            wait(a, s_col, 16)
            with a.Fori(0, KT // 2) as i:
                for e in range(2):
                    a.wait_ge(unit_done, 4 * i + 2 * e + 2)
                    act_fn(t2[:, e, :], ps[:, 2 * e + 1, :], ACT.Sigmoid,
                           bias=col[:, bass.ds(COL["b_gate"][0] + 2 * i + e, 1)]).then_inc(sig_done, 1)
                    norm_hi(2 * i + e + 1, 2 * i + e, [("g_mlp0", act)])

            def mlp(layer):
                n0 = H_MLP[layer]
                root(0 if layer == 0 else 2)

                def hidden(b, par):
                    for m in range(KT):
                        n = NB_FF * KT * layer + KT * b + m
                        a.wait_ge(hid_sq, n + 1)
                        act_fn(hid[:, par, 0, m, :], t2[:, m % 2, :], ACT.Copy).then_inc(hid_hi, 1)

                with a.Fori(0, NB_FF // 2) as i:
                    hidden(2 * i, 0)
                    hidden(2 * i + 1, 1)
                if layer == 0:
                    with a.Fori(0, KT) as m:
                        norm_hi(n0 + (NB_FF - 1) * KT + 1 + m, m, [("g_kv", act), ("g_q", hid[:, 0])])

            mlp(0)
            root(1)
            wait(a, stat_c, 2)
            act_fn(rcol[:], scol[:], ACT.Sqrt).then_inc(stat_a, 1)

            def stage(n, u):
                q = u % 2
                Q = QUADS * n + u
                wait(a, q_done, KT)
                wait(a, pads, 1)
                wait(a, s_mm, Q - 1)
                for e in range(2):
                    r = slice(64 * e, 64 * e + 64)
                    act_fn(qstage[r, q, e:e + 3:2, :], qT[r, 2 * u:2 * u + 2, bass.ds(n * BLK, BLK)],
                           ACT.Copy, scale=HD ** -0.5).then_inc(q_staged, 1)

            def exps(n, u):
                q = u % 2
                Q = QUADS * n + u
                a.wait_ge(m_step, 4 * Q + 4)
                act_fn(es[:, q, :], sm[:, q, :], ACT.Exp).then_inc(es_done, 1)
                for i in range(4):
                    act_fn(s_sb[:, q, i, :], s_sb[:, q, i, :], ACT.Exp, bias=negm[:, q, i:i + 1],
                           accum_out=den[:, q, i:i + 1]).then_inc(p_exp, 1)

            def turned(n, u):
                q = u % 2
                Q = QUADS * n + u
                a.wait_ge(pt_mm, Q + 1)
                act_fn(pT[:, q, 0:2].rearrange("p i b n -> p (i b n)"), ps[:, 4, :], ACT.Copy).then_inc(pt_a, 1)

            def o_hi(n, u):
                q = u % 2
                Q = QUADS * n + u
                a.wait_ge(ot_mm, Q + 1)
                act_fn(hid[:, 0, 0, 2 * u:2 * u + 2, bass.ds(n * BLK, BLK)],
                       ps[:, 7, q * 256:q * 256 + 256].rearrange("p (t n) -> p t n", t=2),
                       ACT.Copy).then_inc(ot_hi, 1)

            skewed(a, [(turned, 2), (stage, -1), (o_hi, 3), (exps, 0)], lambda: stage(0, 0))

            with a.Fori(0, KT) as m:
                norm_hi(H_O + 1 + m, m, [("g_mlp1", act)])
            mlp(1)
            root(3)

        @block.vector
        def _(v):
            tt, ts, stt = nc.vector.tensor_tensor, nc.vector.tensor_scalar, nc.vector.scalar_tensor_tensor
            count = [0]

            def link(ins):
                count[0] += 1
                ins.then_inc(setup_v, 1)
                v.wait_ge(setup_v, count[0])

            def sm_(i):
                return small[:, i]

            def turns(dst, tmp):
                link(ts(tmp, dst, ROUND, ROUND, ALU.add, ALU.subtract))
                link(tt(dst, dst, tmp, ALU.subtract))

            nc.vector.memset(acc[:], 0.0).then_inc(sq_acc, 1)
            nc.vector.memset(stat[:], 0.0).then_inc(bank_free, 4)
            wait(v, s_lam, 16)
            wait(v, s_cst, 16)
            re, im = sm_(1), PR("a_im")
            link(ts(re, PR("a_re"), LAM_MAX, None, ALU.min))
            wait(v, setup_a, 1)
            link(tt(sm_(2), im, sm_(0), ALU.mult))
            link(tt(sm_(3), re, sm_(0), ALU.mult))
            power = C_("pow").unsqueeze(1).to_broadcast([P, GP, NPOW])
            link(tt(mag[:], sm_(3).unsqueeze(2).to_broadcast([P, GP, NPOW]), power, ALU.mult))
            assert count[0] == SETUP_EXP
            link(ts(sm_(2), sm_(2), 1.0 / (2.0 * np.pi), None, ALU.mult))
            turns(sm_(2), sm_(5))
            link(tt(ph[:], sm_(2).unsqueeze(2).to_broadcast([P, GP, NPOW]), power, ALU.mult))
            turns(ph[:], rnd[:])
            assert count[0] == SETUP_PH
            link(ts(sm_(6), sm_(2), float(J), None, ALU.mult))
            turns(sm_(6), sm_(5))
            wait(v, setup_a, 5)
            link(ts(sm_(7), sm_(4), -1.0, 1.0, ALU.mult, ALU.add))
            link(nc.vector.reciprocal(sm_(7), sm_(7)))
            link(stt(sm_(7), sm_(4), 2.0, sm_(7), ALU.mult, ALU.mult))
            sh1 = l_re[:, :, 1:2].rearrange("p g a -> p (g a)")
            link(stt(sm_(8), sh1, -2.0, sh1, ALU.mult, ALU.mult))
            link(stt(sm_(9), sm_(8), 1.0, sm_(7), ALU.add, ALU.mult))
            link(tt(sm_(9), sm_(9), sm_(8), ALU.add))
            link(tt(l_re[:], l_re[:], l_re[:], ALU.mult))
            link(ts(l_re[:], l_re[:], -2.0, 1.0, ALU.mult, ALU.add))
            link(tt(l_re[:], l_re[:], mag[:], ALU.mult))
            link(tt(l_im[:], l_im[:], mag[:], ALU.mult))
            link(ts(nl_re[:], l_re[:, :, 0:J + 1], -1.0, None, ALU.mult))
            link(ts(nl_im[:], l_im[:, :, 0:J + 1], -1.0, None, ALU.mult))
            assert count[0] == SETUP_POW
            li1 = l_im[:, :, 1:2].rearrange("p g a -> p (g a)")
            link(tt(sm_(5), re, re, ALU.mult))
            link(tt(sm_(10), im, im, ALU.mult))
            link(tt(sm_(5), sm_(5), sm_(10), ALU.add))
            link(nc.vector.reciprocal(sm_(5), sm_(5)))
            link(tt(sm_(10), sm_(9), re, ALU.mult))
            link(tt(sm_(11), li1, im, ALU.mult))
            link(tt(sm_(10), sm_(10), sm_(11), ALU.add))
            link(tt(sm_(10), sm_(10), sm_(5), ALU.mult))
            link(tt(sm_(12), li1, re, ALU.mult))
            link(tt(sm_(13), sm_(9), im, ALU.mult))
            link(tt(sm_(12), sm_(12), sm_(13), ALU.subtract))
            link(tt(sm_(12), sm_(12), sm_(5), ALU.mult))
            f_re = sm_(10).unsqueeze(2).to_broadcast([P, GP, J])
            f_im = sm_(12).unsqueeze(2).to_broadcast([P, GP, J])
            lr, li = l_re[:, :, J + 1:], l_im[:, :, J + 1:]
            tmp = rnd[:, :, 0:J]
            link(tt(x_re[:], lr, f_re, ALU.mult))
            link(tt(tmp, li, f_im, ALU.mult))
            link(tt(x_re[:], x_re[:], tmp, ALU.subtract))
            link(tt(x_im[:], lr, f_im, ALU.mult))
            link(tt(tmp, li, f_re, ALU.mult))
            link(tt(x_im[:], x_im[:], tmp, ALU.add))

            wait(v, sq_used, NO)
            link(nc.vector.tensor_reduce(rstd_u[:, 0], ps[:, 7, :].rearrange("p (g k) -> p k g", k=NK), AX.X, ALU.add))
            link(ts(rstd_u[:, 0], rstd_u[:, 0], 1.0 / D, EPS, ALU.mult, ALU.add))
            link(nc.vector.reciprocal(rstd_u[:, 1], rstd_u[:, 0]))
            assert count[0] == SETUP_MS
            wait(v, setup_a, 6)
            wait(v, s_dd, 16)
            wait(v, s_prm, 16)

            def frame(c):
                pairs = bass.ds(8 * c, 8)
                wait(v, frame_a, 2 * c)
                tt(phk[:], small[:, 6, pairs].unsqueeze(2).to_broadcast([P, 8, NK]),
                   C_("chunk").unsqueeze(1).to_broadcast([P, 8, NK]), ALU.mult).then_inc(frame_v, 1)
                v.wait_ge(frame_v, 5 * c + 1)
                ts(phr[:], phk[:], ROUND, ROUND, ALU.add, ALU.subtract).then_inc(frame_v, 1)
                v.wait_ge(frame_v, 5 * c + 2)
                tt(phk[:], phk[:], phr[:], ALU.subtract).then_inc(frame_v, 1)

            def frame_end(c):
                pairs = bass.ds(8 * c, 8)
                v.wait_ge(frame_a, 2 * c + 2)
                tt(cosk[:, pairs], cosk[:, pairs], cosk[:, pairs], ALU.mult).then_inc(frame_v, 1)
                v.wait_ge(frame_v, 5 * c + 4)
                ts(cosk[:, pairs], cosk[:, pairs], -2.0, 1.0, ALU.mult, ALU.add).then_inc(frame_v, 1)

            def project(o, q):
                def b(name):
                    return prm[:, bass.ds(PRM[name][0] + o * OGP * C, OGP * C)].rearrange(
                        "p (g c) -> p g c", c=C).unsqueeze(2).to_broadcast([P, OGP, J, C])

                def x(table):
                    return table[:, bass.ds(o * OGP, OGP), :].unsqueeze(3).to_broadcast([P, OGP, J, C])

                wait(v, p_done, 2 * o)
                for i, (bb, xx) in enumerate((("b_re", x_re), ("b_im", x_im), ("b_re", x_im), ("b_im", x_re))):
                    tt(p_tmp[:, i], b(bb), x(xx), ALU.mult).then_inc(p_step, 1)

            def project_sum(o, q):
                v.wait_ge(p_step, 4 * o + 4)
                wait(v, k_mm, o - 1)
                tt(p_ri[:, q, 0], p_tmp[:, 0], p_tmp[:, 1], ALU.subtract).then_inc(p_done, 1)
                tt(p_ri[:, q, 1], p_tmp[:, 2], p_tmp[:, 3], ALU.add).then_inc(p_done, 1)

            def inputs(o, q):
                wait(v, u_step, o + 1)
                part = xy[:, bass.ds(o * OCT, OCT), :]
                tt(part, part, rstd_u[:, 0].unsqueeze(1).to_broadcast([P, OCT, NK]), ALU.mult).then_inc(u_done, 1)

            def run_states(o, q):
                cos = cosk[:, bass.ds(o * OGP, OGP), :].rearrange("p g k -> p (g k)").unsqueeze(1).to_broadcast([P, 2, OGP * NK])
                sin = sink_[:, bass.ds(o * OGP, OGP), :].rearrange("p g k -> p (g k)").unsqueeze(1).to_broadcast([P, 2, OGP * NK])

                def flat(t):
                    return t.rearrange("p r g k -> p r (g k)")

                b = ps[:, 4, :].rearrange("p (r n) -> p r n", r=2)
                if isinstance(o, int) and o % 2 == 0:
                    v.wait_ge(frame_v, 5 * (o // 2) + 5)
                wait(v, st_done, 2 * o)
                wait(v, b_mm, o + 1)
                tt(flat(rc[:]), b, cos, ALU.mult).then_inc(rot, 1)
                tt(flat(rs[:]), b, sin, ALU.mult).then_inc(b_read, 1)
                v.wait_ge(rot, 6 * o + 1)
                v.wait_ge(b_read, o + 1)
                tt(rb[:, 0], rc[:, 0], rs[:, 1], ALU.add).then_inc(rot, 1)
                tt(rb[:, 1], rc[:, 1], rs[:, 0], ALU.subtract).then_inc(rot, 1)
                v.wait_ge(rot, 6 * o + 3)
                v.wait_ge(w_done, 2 * o + 2)
                nc.vector.tensor_tensor_scan(rb[:].rearrange("p r g k -> p (r g k)"),
                                             decay[:, q].rearrange("p r g k -> p (r g k)"),
                                             rb[:].rearrange("p r g k -> p (r g k)"),
                                             0.0, ALU.mult, ALU.add).then_inc(rot, 1)
                v.wait_ge(rot, 6 * o + 4)
                tt(flat(rc[:]), flat(rb[:]), cos, ALU.mult).then_inc(rot, 1)
                tt(flat(rs[:]), flat(rb[:]), sin, ALU.mult).then_inc(rot, 1)
                v.wait_ge(rot, 6 * o + 6)
                wait(v, zeroed, 3)
                wait(v, y_mm, o - 1)
                tt(st[:, q, 0, :, 1:], rc[:, 0], rs[:, 1], ALU.subtract).then_inc(st_done, 1)
                tt(st[:, q, 1, :, 1:], rs[:, 0], rc[:, 1], ALU.add).then_inc(st_done, 1)
                wait(v, k_evac, o + 1)
                tt(k_out[:, :, :, 0:C], k_out[:, :, :, 0:C],
                   ddiag[:, :, bass.ds(o * OGP, OGP), :], ALU.add).then_inc(k_diag, 1)

            octets(v, [(project_sum, -1), (inputs, -1), (project, -2), (run_states, 0)], frame, frame_end)

            for o in range(NO):
                wait(v, y_hi, o + 1)
                tt(hid[:, 0, 1, o, :], xy[:, o * OCT:(o + 1) * OCT, :].rearrange("p g k -> p (g k)"),
                   hid[:, 0, 0, o, :].bitcast(F32), ALU.subtract).then_inc(y_lo, 1)

            def tile(t, m):
                return t[:, bass.ds(m, 1), :].rearrange("p a n -> p (a n)")

            def normed(added, norm, n_base, m, outs):
                v.wait_ge(h_added, added)
                tt(t1[:], tile(h, m), tile(h, m), ALU.mult).then_inc(sq_tmp, 1)
                v.wait_ge(sq_tmp, norm * KT + m + 1)
                v.wait_ge(sq_acc, norm * (KT + 1) + m + 1)
                tt(acc[:], acc[:], t1[:], ALU.add).then_inc(sq_acc, 1)
                for i, (g, dst) in enumerate(outs):
                    v.wait_ge(n_hi, n_base + i + 1)
                    stt(tile(dst[:, 1], m), tile(h, m), col[:, bass.ds(COL[g][0] + m, 1)],
                        tile(dst[:, 0], m).bitcast(F32), ALU.mult, ALU.subtract).then_inc(n_lo, 1)

            def inverse(n, cols=False):
                wait(v, stat_mm, n + 1)
                if cols:
                    wait(v, stat_col_mm, 1)
                ts(stat[:], ps[:, 7, :], 1.0 / D, EPS, ALU.mult, ALU.add).then_inc(stat_v, 1)
                if cols:
                    ts(scol[:], ps[:, 6, 0:NBLK], 1.0 / D, EPS, ALU.mult, ALU.add).then_inc(stat_c, 1)
                wait(v, stat_v, 2 * n + 1)
                nc.vector.reciprocal(stat[:], stat[:]).then_inc(stat_v, 1)
                nc.vector.memset(acc[:], 0.0).then_inc(sq_acc, 1)
                if cols:
                    v.wait_ge(stat_c, 1)
                    nc.vector.reciprocal(scol[:], scol[:]).then_inc(stat_c, 1)

            wait(v, s_h, 16)
            wait(v, s_col, 16)
            with v.Fori(0, KT // 2) as i:
                for e in range(2):
                    m = 2 * i + e
                    v.wait_ge(sig_done, m + 1)
                    v.wait_ge(sq_acc, m + 1)
                    stt(t1[:], ps[:, 2 * e, :], col[:, bass.ds(COL["b_val"][0] + m, 1)], t2[:, e, :],
                        ALU.add, ALU.mult).then_inc(bank_free, 2)
                    v.wait_ge(bank_free, 4 + 2 * m + 2)
                    hv = tile(h, m).rearrange("p (k j) -> p j k", j=J)
                    tt(hv, t1[:].rearrange("p (j k) -> p j k", j=J), hv, ALU.add).then_inc(h_added, 1)
                    normed(m + 1, 0, m, m, [("g_mlp0", act)])

            def mlp(layer):
                base, n0, norm = U_MLP[layer], H_MLP[layer], 2 * layer
                inverse(norm)
                wait(v, stat_a, STAT_A[norm])

                def hidden(b, par):
                    for m in range(KT):
                        U = base + m + (0 if isinstance(b, int) and b == 0 else 2 * KT * b - KT)
                        n = NB_FF * KT * layer + KT * b + m
                        v.wait_ge(unit_done, U + 1)
                        stt(t1[:], ps[:, m % 4, :], 0.0, rstd[:], ALU.max, ALU.mult).then_inc(bank_free, 1)
                        v.wait_ge(bank_free, 4 + U + 1)
                        tt(t2[:, m % 2, :], t1[:], t1[:], ALU.mult).then_inc(hid_sq, 1)
                        v.wait_ge(hid_hi, n + 1)
                        tt(hid[:, par, 1, m, :], t2[:, m % 2, :], hid[:, par, 0, m, :].bitcast(F32),
                           ALU.subtract).then_inc(hid_lo, 1)

                def output(b, last):
                    U0 = base + 2 * KT * b + (KT if last else 2 * KT)
                    a0 = n0 + KT * b
                    with v.Fori(0, KT // 4) as i:
                        for s in range(4):
                            m = 4 * i + s
                            v.wait_ge(unit_done, U0 + 1 + m)
                            v.wait_ge(h_added, a0 + m)
                            tt(tile(h, m), ps[:, s, :], tile(h, m), ALU.add).then_inc(bank_free, 1)
                            v.wait_ge(bank_free, 4 + U0 + 1 + m)
                            v.sem_inc(h_added, 1)
                            if last and layer == 0:
                                normed(a0 + m + 1, 1, KT + 2 * m, m, [("g_kv", act), ("g_q", hid[:, 0])])
                            elif last:
                                normed(a0 + m + 1, 3, 4 * KT, m, [])

                hidden(0, 0)
                with v.Fori(0, NB_FF // 2 - 1) as i:
                    hidden(2 * i + 1, 1)
                    output(2 * i, False)
                    hidden(2 * i + 2, 0)
                    output(2 * i + 1, False)
                hidden(NB_FF - 1, 1)
                output(NB_FF - 2, False)
                output(NB_FF - 1, True)

            mlp(0)

            inverse(1, cols=True)
            wait(v, stat_a, STAT_A[1])
            nc.vector.memset(kT[:, :, 0:BLK], 0.0).then_inc(pads, 1)
            nc.vector.memset(v_sb[:, 0, :], 0.0).then_inc(pads, 1)
            for t in range(2):
                wait(v, unit_done, U_KV + t + 1)
                wait(v, kv_done, t)
                tt(t1[:], ps[:, t, :], rstd[:], ALU.mult).then_inc(bank_free, 1)
                wait(v, bank_free, 4 + U_KV + t + 1)
                ts(kT[:, t, BLK:], t1[:], COLS("b_k")[:, t:t + 1], None, ALU.add).then_inc(kv_done, 1)
            for t in range(2):
                wait(v, unit_done, U_KV + 2 + t + 1)
                for n in range(NBLK):
                    ins = stt(v_sb[:, 1 + n, t * P:(t + 1) * P], ps[:, 2 + t, n * P:(n + 1) * P], rcol[:, n:n + 1],
                              COLS("b_v")[:, t * P:(t + 1) * P], ALU.mult, ALU.add)
                    ins.then_inc(kv_done, 1)
                v.wait_ge(kv_done, 2 + 4 * (t + 1))
                v.sem_inc(bank_free, 1)
            wait(v, kv_done, 10)
            nc.vector.memset(qstage[:], 0.0).then_inc(pads, 1)
            with v.Fori(0, KT // 4) as i:
                for s in range(4):
                    m = 4 * i + s
                    v.wait_ge(unit_done, U_Q + 1 + m)
                    tt(t1[:], ps[:, s, :], rstd[:], ALU.mult).then_inc(bank_free, 1)
                    v.wait_ge(bank_free, 4 + U_Q + 1 + m)
                    ts(tile(qT, m), t1[:], col[:, bass.ds(COL["b_q"][0] + m, 1)], None, ALU.add).then_inc(q_done, 1)
                    v.wait_ge(q_done, m + 1)
            wait(v, s_mask, 16)

            def maxima(n, u):
                q = u % 2
                Q = QUADS * n + u
                sink = COLS("sink")[:, 4 * u:4 * u + 4]
                v.wait_ge(s_mm, Q + 1)
                tt(s_sb[:, q], ps[:, 2 * q:2 * q + 2, :].rearrange("p a (i n) -> p (a i) n", n=2 * BLK),
                   mask[:, bass.ds(n, 1), :].to_broadcast([P, 4, 2 * BLK]), ALU.add).then_inc(s_masked, 1)
                v.wait_ge(s_masked, Q + 1)
                nc.vector.tensor_reduce(mx[:, q], s_sb[:, q], AX.X, ALU.max).then_inc(m_step, 1)
                v.wait_ge(m_step, 4 * Q + 1)
                tt(mx[:, q], mx[:, q], sink, ALU.max).then_inc(m_step, 1)
                v.wait_ge(m_step, 4 * Q + 2)
                ts(negm[:, q], mx[:, q], -1.0, None, ALU.mult).then_inc(m_step, 1)
                tt(sm[:, q], sink, mx[:, q], ALU.subtract).then_inc(m_step, 1)

            def denominators(n, u):
                q = u % 2
                Q = QUADS * n + u
                v.wait_ge(p_exp, 4 * Q + 4)
                tt(den[:, q], den[:, q], es[:, q], ALU.add).then_inc(den_done, 1)
                v.wait_ge(den_done, Q + 1)
                nc.vector.reciprocal(rden[:, q], den[:, q]).then_inc(rden_done, 1)

            def turned(n, u):
                q = u % 2
                Q = QUADS * n + u
                v.wait_ge(pt_mm, Q + 1)
                ts(pT[:, q, 2:4].rearrange("p i b n -> p (i b n)"), ps[:, 5, :], 1.0, None, ALU.mult).then_inc(pt_v, 1)

            def normalize(n, u):
                q = u % 2
                Q = QUADS * n + u
                v.wait_ge(o_mm, Q + 1)
                v.wait_ge(rden_done, Q + 1)
                tt(o_sb[:, q], ps[:, 6, q * 256:q * 256 + 256].rearrange("p (i d) -> p i d", d=HD),
                   rden[:, q].unsqueeze(2).to_broadcast([P, 4, HD]), ALU.mult).then_inc(o_norm, 1)

            def o_low(n, u):
                q = u % 2
                Q = QUADS * n + u
                v.wait_ge(ot_hi, Q + 1)
                tt(hid[:, 0, 1, 2 * u:2 * u + 2, bass.ds(n * BLK, BLK)],
                   ps[:, 7, q * 256:q * 256 + 256].rearrange("p (t n) -> p t n", t=2),
                   hid[:, 0, 0, 2 * u:2 * u + 2, bass.ds(n * BLK, BLK)].bitcast(F32),
                   ALU.subtract).then_inc(ot_lo, 1)

            skewed(v, [(turned, 2), (maxima, 0), (normalize, 2), (denominators, 1), (o_low, 3)])

            with v.Fori(0, KT // 4) as i:
                for s in range(4):
                    m = 4 * i + s
                    v.wait_ge(unit_done, U_O + 1 + m)
                    stt(tile(h, m), ps[:, s, :], col[:, bass.ds(COL["b_o"][0] + m, 1)], tile(h, m),
                        ALU.add, ALU.add).then_inc(bank_free, 1)
                    v.wait_ge(bank_free, 4 + U_O + 1 + m)
                    v.sem_inc(h_added, 1)
                    normed(H_O + m + 1, 2, 3 * KT + m, m, [("g_mlp1", act)])

            mlp(1)
            inverse(3)
            wait(v, stat_a, STAT_A[3])
            for m in range(KT):
                stt(h[:, m, :], h[:, m, :], COLS("g_out")[:, m:m + 1], rstd[:], ALU.mult, ALU.mult).then_inc(out_t, 1)

        @block.tensor
        def _(pe):
            mm, turn = nc.tensor.matmul, nc.tensor.transpose

            wait(pe, s_cst, 16)
            for o in range(NO):
                wait(pe, sq_ready, o + 1)
                mm(ps[:, 7, :], C_("same_step"), y_sb[:, o % 2, :], start=(o == 0), stop=(o == NO - 1)
                   ).then_inc(sq_used, 1)

            def fold(o, q):
                wait(pe, p_done, 2 * o + 2)
                wait(pe, v_evac, o)
                for ri in range(2):
                    for g in range(OGP):
                        last = turn(ps[:, ri, g * P:(g + 1) * P], p_ri[:, q, ri, g].rearrange("p j c -> p (j c)"), ident)
                last.then_inc(t_mm, 1)

            def sums(o, q):
                wait(pe, v_evac, o + 1)
                wait(pe, u_copied, o + 1)
                wait(pe, b_read, o)
                for g in range(OGP):
                    for e in range(2):
                        for ri in range(2):
                            last = mm(ps[64 * e:64 * e + 64, 4, (ri * OGP + g) * NK:(ri * OGP + g + 1) * NK],
                                      v_ri[:, q, ri, g, 64 * e:64 * e + 64], u_sb[:, q, 2 * g + e, :],
                                      start=True, stop=True)
                last.then_inc(b_mm, 1)

            def lags(o, q):
                wait(pe, w_done, 2 * o + 1)
                wait(pe, k_evac, o)
                pe.sem_inc(passed, 1)
                for g in range(OGP):
                    for e in range(2):
                        r = slice(64 * e, 64 * e + 64)
                        for ri in range(2):
                            last = mm(ps[0:C, 2 + e, g * P:(g + 1) * P], p_ri[r, q, ri, g, J - 1, :],
                                      w_k[r, ri, g, 0:J, :].rearrange("p j c -> p (j c)"),
                                      start=(ri == 0), stop=(ri == 1))
                last.then_inc(k_mm, 1)

            def outputs(o, q):
                wait(pe, t_in[q], 16 * J * (o // 2 + 1))
                wait(pe, st_done, 2 * o + 2)
                wait(pe, w_copied, o + 1)
                wait(pe, y_evac, 2 * o)
                for g in range(OGP):
                    for e in range(2):
                        r = slice(64 * e, 64 * e + 64)
                        gg = 2 * g + e
                        out = ps[0:NK, 5 + e, g * P:(g + 1) * P]
                        mm(out, u_sb[:, q, gg, :], toep[:, q, e, g, :], start=True, stop=False)
                        for ri in range(2):
                            last = mm(out, st[r, q, ri, g, 0:NK],
                                      w_ri[r, q, ri, g, 1:J + 1, :].rearrange("p j c -> p (j c)"),
                                      start=False, stop=(ri == 1))
                last.then_inc(y_mm, 1)

            def turn_y(o, q):
                wait(pe, y_evac, 2 * o + 2)
                wait(pe, gelu_done, o)
                pe.sem_inc(passed, 1)
                for j in range(J):
                    last = turn(ps[:, 7, j * NK:(j + 1) * NK],
                                y_sb[0:NK].rearrange("p a n -> p (a n)")[:, j * P:(j + 1) * P], ident[0:NK, 0:NK])
                last.then_inc(y_turned, 1)

            ahead, here = swapped_first(fold, lags)
            octets(pe, [ahead, (sums, 0), here, (turn_y, 2), (outputs, 1)])

            def unit(U, s, x, ready=None):
                pe.wait_ge(w_split, U + 1)
                pe.wait_ge(bank_free, U + 1)
                for k in range(KT):
                    if ready is not None:
                        wait(pe, ready[0], ready[1] + ready[2] * k)
                    w = slice(k * P, (k + 1) * P)
                    mm(ps[:, s, :], w_hi[:, s, w], x[:, 0, k, :], start=(k == 0), stop=False)
                    mm(ps[:, s, :], w_hi[:, s, w], x[:, 1, k, :], start=False, stop=False)
                    last = mm(ps[:, s, :], w_lo[:, s, w], x[:, 0, k, :], start=False, stop=(k == KT - 1))
                last.then_inc(unit_done, 1)

            def units(n, U0, x, ready=None):
                with pe.Fori(0, n // 4) as i:
                    for s in range(4):
                        unit(U0 + 4 * i + s, s, x, ready)

            def stats(norm):
                wait(pe, sq_acc, (norm + 1) * (KT + 1))
                mm(ps[:, 7, :], ones, acc[:], start=True, stop=True).then_inc(stat_mm, 1)

            def mlp(layer):
                base = U_MLP[layer]
                n_lo0 = 0 if layer == 0 else 3 * KT
                for s in range(4):
                    unit(base + s, s, act, (n_lo, n_lo0 + 1, 1))
                    if s == 0:
                        stats(2 * layer)
                units(4, base + 4, act)

                def second(b, U0, par):
                    pe.wait_ge(hid_lo, NB_FF * KT * layer + KT * b + KT)
                    units(KT, U0, hid[:, par])

                with pe.Fori(0, NB_FF // 2 - 1) as i:
                    units(KT, base + KT + 4 * KT * i, act)
                    second(2 * i, base + 2 * KT + 4 * KT * i, 0)
                    units(KT, base + 3 * KT + 4 * KT * i, act)
                    second(2 * i + 1, base + 4 * KT + 4 * KT * i, 1)
                units(KT, base + (2 * NB_FF - 3) * KT, act)
                second(NB_FF - 2, base + (2 * NB_FF - 2) * KT, 0)
                second(NB_FF - 1, base + (2 * NB_FF - 1) * KT, 1)

            for pair in ((0, 1), (2, 3)):
                pe.wait_ge(w_split, pair[1] + 1)
                pe.wait_ge(bank_free, 4)
                for k in range(KT):
                    wait(pe, y_lo, k + 1)
                    w = slice(k * P, (k + 1) * P)
                    for s in pair:
                        mm(ps[:, s, :], w_hi[:, s, w], hid[:, 0, 0, k, :], start=(k == 0), stop=False)
                        mm(ps[:, s, :], w_hi[:, s, w], hid[:, 0, 1, k, :], start=False, stop=False)
                        last = mm(ps[:, s, :], w_lo[:, s, w], hid[:, 0, 0, k, :], start=False, stop=(k == KT - 1))
                        if k == KT - 1:
                            last.then_inc(unit_done, 1)
            units(2 * KT - 4, U_GLU + 4, hid[:, 0])
            mlp(0)

            for t in range(2):
                unit(U_KV + t, t, act, (n_lo, KT + 1, 2))
                if t == 0:
                    stats(1)
                    for n in range(NBLK):
                        last = mm(ps[:, 6, n:n + 1], acc[:, n * P:(n + 1) * P], ones[:, 0:1], start=True, stop=True)
                    last.then_inc(stat_col_mm, 1)
            for t in range(2):
                s = 2 + t
                wait(pe, w_split, U_KV + s + 1)
                wait(pe, bank_free, U_KV + s + 1)
                for n in range(NBLK):
                    tok = slice(n * P, (n + 1) * P)
                    for k in range(KT):
                        w = slice(k * P, (k + 1) * P)
                        mm(ps[:, s, tok], act[:, 0, k, tok], w_hi[:, s, w], start=(k == 0), stop=False)
                        mm(ps[:, s, tok], act[:, 0, k, tok], w_lo[:, s, w], start=False, stop=False)
                        last = mm(ps[:, s, tok], act[:, 1, k, tok], w_hi[:, s, w], start=False, stop=(k == KT - 1))
                last.then_inc(unit_done, 1)
            units(KT, U_Q, hid[:, 0], (n_lo, KT + 2, 2))

            def scores(n, u):
                q = u % 2
                Q = QUADS * n + u
                wait(pe, q_staged, 2 * Q + 2)
                wait(pe, s_masked, Q - 1)
                wait(pe, kv_done, 10)
                wait(pe, pads, 3)
                if isinstance(n, int) and Q < 2:
                    wait(pe, bank_free, 4 + U_O)
                for i in range(4):
                    last = mm(ps[:, 2 * q + i // 2, (i % 2) * 2 * BLK:(i % 2 + 1) * 2 * BLK], qstage[:, q, i, :],
                              kT[:, u // 2, bass.ds(n * BLK, 2 * BLK)], start=True, stop=True)
                last.then_inc(s_mm, 1)

            def turn_p(n, u):
                q = u % 2
                Q = QUADS * n + u
                pe.wait_ge(p_exp, 4 * Q + 4)
                wait(pe, pt_a, Q)
                wait(pe, pt_v, Q)
                for i in range(4):
                    for b in range(2):
                        at = (i % 2) * 2 * BLK + b * BLK
                        last = turn(ps[:, 4 + i // 2, at:at + BLK], s_sb[:, q, i, b * BLK:(b + 1) * BLK], ident)
                last.then_inc(pt_mm, 1)

            def mix(n, u):
                q = u % 2
                Q = QUADS * n + u
                pe.wait_ge(pt_a, Q + 1)
                pe.wait_ge(pt_v, Q + 1)
                wait(pe, o_norm, Q)
                for i in range(4):
                    kvh = 2 * (u // 2) + i % 2
                    for b in range(2):
                        last = mm(ps[:, 6, q * 256 + i * HD:q * 256 + (i + 1) * HD], pT[:, q, i, b, :],
                                  v_sb[:, bass.ds(n + b, 1), kvh * HD:(kvh + 1) * HD].rearrange("p a d -> p (a d)"),
                                  start=(b == 0), stop=(b == 1))
                last.then_inc(o_mm, 1)

            def turn_o(n, u):
                q = u % 2
                Q = QUADS * n + u
                pe.wait_ge(o_norm, Q + 1)
                wait(pe, ot_lo, Q)
                for t in range(2):
                    last = turn(ps[:, 7, q * 256 + t * P:q * 256 + (t + 1) * P],
                                o_sb[:, q, 2 * t:2 * t + 2, :].rearrange("p e d -> p (e d)"), ident)
                last.then_inc(ot_mm, 1)

            skewed(pe, [(scores, 0), (mix, 2), (turn_o, 3), (turn_p, 1)])

            pe.wait_ge(ot_lo, QUADS * NBLK)
            units(KT, U_O, hid[:, 0])
            mlp(1)
            stats(3)


def skewed(eng, stages, before=None):
    last = QUADS * NBLK
    longest = max(lag for _, lag in stages)
    if before:
        before()
    for Q in range(QUADS):
        for stage, lag in stages:
            if Q - lag >= 0:
                stage((Q - lag) // QUADS, (Q - lag) % QUADS)
    with eng.Fori(1, NBLK - 1) as n:
        for u in range(QUADS):
            for stage, lag in stages:
                stage(n + (u - lag) // QUADS, (u - lag) % QUADS)
    for Q in range(last - QUADS, last + longest):
        for stage, lag in stages:
            if Q - lag < last:
                stage((Q - lag) // QUADS, (Q - lag) % QUADS)


def _feature_rows(a):
    return a.T.reshape(KT, P, L).transpose(1, 0, 2)


def _panels(w):
    n = w.shape[1] // P
    return w.reshape(KT, P, n, P).transpose(2, 1, 0, 3).reshape(n, P, KT * P)


def kernel(**inputs):
    from concourse import bacc
    from concourse.bass_utils import run_bass_kernel_spmd

    f = {k: np.asarray(v) for k, v in inputs.items()}
    x = f["x"][0]

    def states(a):
        a = a.reshape((GP, 2, S) + a.shape[2:])
        return np.moveaxis(a, 0, 2).reshape((P, GP) + a.shape[3:])

    def cols(a):
        return a.reshape(-1, P).T

    def rows(a):
        return np.broadcast_to(a, (P, a.size))

    group = NQ // NKV
    heads = [(2 * (t // group) + e) * group + t % group for t in range(NQ // 2) for e in range(2)]

    panels = []
    glu = _panels(f["s5_w_glu"][0])
    for m in range(KT):
        panels += [glu[m], glu[KT + m]]

    def mlp(layer):
        w_in = _panels(f["w_mlp_in"][layer])
        w_out = [_panels(f["w_mlp_out"][layer][b * D:(b + 1) * D]) for b in range(NB_FF)]
        order = [w_in[0:KT]]
        for b in range(1, NB_FF):
            order += [w_in[b * KT:(b + 1) * KT], w_out[b - 1]]
        order.append(w_out[NB_FF - 1])
        return [p for block in order for p in block]

    panels += mlp(0)
    panels += list(_panels(f["w_kv"]))
    panels += list(_panels(f["w_q"][0].reshape(D, NQ, HD)[:, heads].reshape(D, D)))
    panels += list(_panels(f["w_o"][0].reshape(NQ, HD, D)[heads].reshape(D, D)))
    panels += mlp(1)

    g_in = np.broadcast_to(f["norm_mix"][0].reshape(G, C).T[None], (J, C, G)).reshape(P, G)
    prm = np.concatenate([
        states(f["s5_a_re"][0]), states(f["s5_a_im"][0]),
        states(np.broadcast_to(f["s5_log_dt"][0][:, None], (G, S))),
        states(f["s5_b_re"][0]).reshape(P, -1), states(f["s5_b_im"][0]).reshape(P, -1),
        states(f["s5_c_re"][0].transpose(0, 2, 1)).reshape(P, -1),
        states(f["s5_c_im"][0].transpose(0, 2, 1)).reshape(P, -1), g_in], axis=1)
    skip = f["s5_d"][0].reshape(GP, 2, C)
    ddiag = np.zeros((C, 2, GP, C), np.float32)
    for c in range(C):
        ddiag[c, :, :, c] = skip[:, :, c].T
    b_kv, b_glu = f["b_kv"], f["s5_b_glu"][0]
    col = np.concatenate([
        cols(b_glu[:D]), cols(b_glu[D:]), cols(f["norm_mlp"][0]), cols(f["norm_kv"]), cols(f["norm_mix"][1]),
        cols(f["norm_mlp"][1]), cols(f["norm_final"]), cols(b_kv[:NKV * HD]),
        cols(f["b_q"][0].reshape(NQ, HD)[heads].reshape(-1)), cols(f["b_o"][0]), rows(b_kv[NKV * HD:]),
        rows(f["sinks"][0][heads])], axis=1)

    keep = np.ones(NK)
    keep[0] = 0
    step = np.arange(P) // C
    cst = np.concatenate([
        rows(np.concatenate([np.arange(J + 1), np.arange(J)[::-1]])), rows(np.arange(NK)), rows(keep),
        step[:, None] == step[None, :], np.eye(P), np.ones((P, P))], axis=1).astype(np.float32)
    back = np.arange(BLK)[:, None] + BLK - np.arange(2 * BLK)[None, :]
    inside = (back >= 0) & (back < BLK)
    first = inside & (np.arange(2 * BLK) >= BLK)[None, :]
    mask = np.where(np.stack([first] + [inside] * (NBLK - 1), axis=1), 0.0, -1e30).astype(np.float32)

    arrays = {
        "panels": np.stack(panels),
        "xu": x.reshape(NK, J, G, C).transpose(1, 3, 2, 0).reshape(P, G, NK),
        "x_rows": _feature_rows(x), "prm": prm, "ddiag": ddiag, "cst": cst, "mask": mask, "col": col,
    }
    arrays = {k + "_in": np.ascontiguousarray(v) for k, v in arrays.items()}
    nc = bacc.Bacc("TRN2", target_bir_lowering=False, num_devices=1)
    aps = [nc.dram_tensor(k, v.shape, F32, kind="ExternalInput").ap() for k, v in arrays.items()]
    out = nc.dram_tensor("out", (KT, P, L), F32, kind="ExternalOutput").ap()
    build(nc, *aps, out)
    r = run_bass_kernel_spmd(nc, [arrays], core_ids=[0])
    return r.results[0]["out"].transpose(2, 0, 1).reshape(1, L, D)
```

```python
from contextlib import ExitStack

import numpy as np

import concourse.bass as bass
from concourse import mybir

F32 = mybir.dt.float32
F32R = mybir.dt.float32r
ALU = mybir.AluOpType
ACT = mybir.ActivationFunctionType
AX = mybir.AxisListType

P = 128
D = 1024
L = 512
KT = D // P
FF = 4 * D
NB_FF = FF // D
EPS = 1e-5
J = 8
NK = L // J
C = 16
G = D // C
S = 64
GP = G // 2
OCT = 8
NO = G // OCT
OGP = OCT // 2
HD = 64
NQ = 16
NKV = 4
BLK = 128
NBLK = L // BLK
QUADS = 4
LAM_MAX = -1e-4

U_GLU = 0
U_MLP = (U_GLU + 2 * KT, U_GLU + 2 * KT + 2 * NB_FF * KT + 4 + 2 * KT)
U_KV = U_MLP[0] + 2 * NB_FF * KT
U_Q = U_KV + 4
U_O = U_Q + KT
NU = U_MLP[1] + 2 * NB_FF * KT
assert U_O + KT == U_MLP[1] and U_GLU == 0

PRM = {}
_at = 0
for _name, _n in (("a_re", GP), ("a_im", GP), ("log_dt", GP), ("b_re", GP * C), ("b_im", GP * C),
                  ("c_re", GP * C), ("c_im", GP * C), ("g_in", G)):
    PRM[_name] = (_at, _at + _n)
    _at += _n
N_PRM = _at
N_LAM = PRM["log_dt"][1]
NPOW = (J + 1) + J
CST = {}
_at = 0
for _name, _n in (("pow", NPOW), ("chunk", NK), ("keep", NK), ("same_step", P), ("ident", P), ("ones", P)):
    CST[_name] = (_at, _at + _n)
    _at += _n
N_CST = _at
COL = {}
_at = 0
for _name, _n in (("b_val", KT), ("b_gate", KT), ("g_mlp0", KT), ("g_kv", KT), ("g_q", KT), ("g_mlp1", KT),
                  ("g_out", KT), ("b_k", 2), ("b_q", KT), ("b_o", KT), ("b_v", NKV * HD), ("sink", NQ)):
    COL[_name] = (_at, _at + _n)
    _at += _n
N_COL = _at

H_MLP = (KT, KT + NB_FF * KT + KT)
H_O = KT + NB_FF * KT
SETUP_EXP, SETUP_PH, SETUP_POW, SETUP_MS = 4, 10, 25, 46
STAT_A = (1, 3, 4, 5)

TWO_PI = 6.283185
PI_ = 3.1415925
ROUND = 1.5 * 2.0 ** 23


def build(nc, panels, xu_d, x_d, prm_d, ddiag_d, cst_d, mask_d, col_d, out_d):
    ctx = ExitStack()
    with ctx:
        def sb(name, shape, dt=F32, where=ctx):
            return where.enter_context(nc.sbuf_tensor(name, shape, dt))

        def sem(name):
            return ctx.enter_context(nc.semaphore(name))

        h = sb("h", [P, KT, L])
        raw = sb("raw", [P, 2, D])
        early = ExitStack()
        w_tmp = sb("w_tmp", [P, 4, OGP, J + 1, C], where=early)
        p_tmp = sb("p_tmp", [P, 4, OGP, J, C], where=early)
        early.close()
        w_hi = sb("w_hi", [P, 4, D], F32R)
        w_lo = sb("w_lo", [P, 4, D], F32R)
        cst = sb("cst", [P, N_CST])
        col = sb("col", [P, N_COL])
        acc = sb("acc", [P, L])
        rstd = sb("rstd", [P, L])
        rcol = sb("rcol", [P, NBLK])
        stat = sb("stat", [P, L])
        scol = sb("scol", [P, NBLK])
        gate_sb = sb("gate_sb", [P, 2])
        t1 = sb("t1", [P, L])
        t2 = sb("t2", [P, 2, L])

        s5 = ExitStack()
        prm = sb("prm", [P, N_PRM], where=s5)
        ddiag = sb("ddiag", [C, 2, GP, C], where=s5)
        small = sb("small", [P, 16, GP], where=s5)
        ph = sb("ph", [P, GP, NPOW], where=s5)
        mag = sb("mag", [P, GP, NPOW], where=s5)
        rnd = sb("rnd", [P, GP, NPOW], where=s5)
        l_im = sb("l_im", [P, GP, NPOW], where=s5)
        l_re = sb("l_re", [P, GP, NPOW], where=s5)
        nl_re = sb("nl_re", [P, GP, J + 1], where=s5)
        nl_im = sb("nl_im", [P, GP, J + 1], where=s5)
        x_re = sb("x_re", [P, GP, J], where=s5)
        x_im = sb("x_im", [P, GP, J], where=s5)
        cosk = sb("cosk", [P, GP, NK], where=s5)
        sink_ = sb("sink_", [P, GP, NK], where=s5)
        phk = t1.rearrange("p (g k) -> p g k", k=NK)
        phr = rstd.rearrange("p (g k) -> p g k", k=NK)
        rstd_u = sb("rstd_u", [P, 2, NK], where=s5)
        p_ri = sb("p_ri", [P, 2, 2, OGP, J, C], where=s5)
        u_sb = sb("u_sb", [P, 2, OCT, NK], where=s5)
        w_k = sb("w_k", [P, 2, OGP, J + 1, C], where=s5)
        w_ri = sb("w_ri", [P, 2, 2, OGP, J + 1, C], where=s5)
        v_ri = sb("v_ri", [P, 2, 2, OGP, P], where=s5)
        k_out = sb("k_out", [C, 2, OGP, P], where=s5)
        p_0 = sb("p_0", [P, 2, OGP, 2, 32], where=s5)
        toep = sb("toep", [P, 2, 2, OGP, P], where=s5)
        decay = sb("decay", [P, 2, 2, OGP, NK], where=s5)
        rc = sb("rc", [P, 2, OGP, NK], where=s5)
        rs = sb("rs", [P, 2, OGP, NK], where=s5)
        rb = sb("rb", [P, 2, OGP, NK], where=s5)
        st = sb("st", [P, 2, 2, OGP, NK + 1], where=s5)
        y_sb = sb("y_sb", [P, 2, OCT * NK], where=s5)
        xy = sb("xy", [P, G, NK], where=s5)
        s5.close()

        hid = sb("hid", [P, 2, 2, KT, L], F32R)
        over = ExitStack()
        act = sb("act", [P, 2, KT, L], F32R, where=over)
        over.close()
        over = ExitStack()
        qT = sb("qT", [P, KT, L], where=over)
        qstage = sb("qstage", [P, 2, 4, BLK], where=over)
        pT = sb("pT", [P, 2, 4, 2, BLK], where=over)
        o_sb = sb("o_sb", [P, 2, 4, HD], where=over)
        fill = sb("fill", [P, 32 * 256 - (KT * L + 2 * 4 * BLK + 2 * 4 * 2 * BLK + 2 * 4 * HD)], where=over)
        kT = sb("kT", [P, 2, BLK + L], where=over)
        v_sb = sb("v_sb", [P, 1 + NBLK, NKV * HD], where=over)
        s_sb = sb("s_sb", [P, 2, 4, 2 * BLK], where=over)
        mask = sb("mask", [P, NBLK, 2 * BLK], where=over)
        mx = sb("mx", [P, 2, 4], where=over)
        negm = sb("negm", [P, 2, 4], where=over)
        sm = sb("sm", [P, 2, 4], where=over)
        es = sb("es", [P, 2, 4], where=over)
        den = sb("den", [P, 2, 4], where=over)
        rden = sb("rden", [P, 2, 4], where=over)
        over.close()

        ps = ctx.enter_context(nc.psum_tensor("ps", [P, 8, 512], F32))

        s_lam, s_prm, s_cst, s_h, s_col, s_mask, s_dd = (sem(n) for n in (
            "lam_in", "prm_in", "cst_in", "h_in", "col_in", "mask_in", "ddiag_in"))
        s_xu = [sem(f"xu_in{c}") for c in range(4)]
        raw_in = [sem("raw_in0"), sem("raw_in1")]
        w_hi_done, w_split = sem("w_hi_done"), sem("w_split")
        unit_done, bank_free = sem("unit_done"), sem("bank_free")
        setup_v, setup_a = sem("setup_v"), sem("setup_a")
        frame_v, frame_a = sem("frame_v"), sem("frame_a")
        sq_ready, sq_used = sem("sq_ready"), sem("sq_used")
        zeroed, passed = sem("zeroed"), sem("passed")
        p_step, p_done, p_copied, w_copied = sem("p_step"), sem("p_done"), sem("p_copied"), sem("w_copied")
        u_step, u_done, u_copied = sem("u_step"), sem("u_done"), sem("u_copied")
        w_step, w_done = sem("w_step"), sem("w_done")
        t_mm, k_mm, b_mm, y_mm = sem("t_mm"), sem("k_mm"), sem("b_mm"), sem("y_mm")
        v_evac, k_evac, k_diag = sem("v_evac"), sem("k_evac"), sem("k_diag")
        b_read, rot, st_done = sem("b_read"), sem("rot"), sem("st_done")
        t_in = [sem("toep_in0"), sem("toep_in1")]
        gelu_done = sem("gelu_done")
        y_evac, y_turned = sem("y_evac"), sem("y_turned")
        y_hi, y_lo = sem("y_hi"), sem("y_lo")
        sig_done = sem("sig_done")
        h_added, sq_tmp, sq_acc = sem("h_added"), sem("sq_tmp"), sem("sq_acc")
        n_hi, n_lo = sem("n_hi"), sem("n_lo")
        stat_mm, stat_v, stat_a = sem("stat_mm"), sem("stat_v"), sem("stat_a")
        stat_col_mm, stat_c, diagonals = sem("stat_col_mm"), sem("stat_c"), sem("diagonals")
        hid_sq, hid_hi, hid_lo = sem("hid_sq"), sem("hid_hi"), sem("hid_lo")
        kv_done, pads = sem("kv_done"), sem("pads")
        q_done = sem("q_done")
        q_staged, s_mm, s_masked, m_step = sem("q_staged"), sem("s_mm"), sem("s_masked"), sem("m_step")
        p_exp, es_done, den_done, rden_done = sem("p_exp"), sem("es_done"), sem("den_done"), sem("rden_done")
        pt_mm, pt_v, pt_a = sem("pt_mm"), sem("pt_v"), sem("pt_a")
        o_mm, o_norm, ot_mm, ot_hi, ot_lo = sem("o_mm"), sem("o_norm"), sem("ot_mm"), sem("ot_hi"), sem("ot_lo")
        out_t, out_s = sem("out_tile"), sem("out_stored")

        def wait(eng, s, value):
            if not (isinstance(value, int) and value <= 0):
                eng.wait_ge(s, value)

        def C_(name):
            a, b = CST[name]
            return cst[:, a:b]

        def COLS(name):
            a, b = COL[name]
            return col[:, a:b]

        def PR(name):
            a, b = PRM[name]
            return prm[:, a:b]

        def octets(eng, stages, late={}):
            def step(o, par, c):
                for stage, lag in stages:
                    if lag in ("begin", "end"):
                        if c.get(lag) is not None:
                            stage(c[lag])
                    elif not isinstance(o, int) or 0 <= o - lag < NO:
                        stage(o - lag, (par - lag) % 2)

            for o in range(-2, 2):
                step(o, o, {"begin": 1} if o == 1 else {})
            with eng.Fori(1, NO // 2 - 1) as i:
                step(2 * i, 0, {"end": i})
                step(2 * i + 1, 1, {"begin": i + 1})
            for o in range(NO - 2, NO + 2):
                if o in late:
                    late[o]()
                step(o, o, {"end": o // 2} if o == NO - 2 else {})

        ident, ones = C_("ident"), C_("ones")
        block = ctx.enter_context(nc.Block())

        @block.sync
        def _(sp):
            sp.dma_start(prm[:, 0:N_LAM], prm_d[:, 0:N_LAM]).then_inc(s_lam, 16)
            sp.dma_start(cst[:], cst_d).then_inc(s_cst, 16)
            for c in range(4):
                part = slice(2 * c * OCT, (2 * c + 2) * OCT)
                sp.dma_start(xy[:, part, :], xu_d[:, part, :]).then_inc(s_xu[c], 16)
            sp.dma_start(prm[:, N_LAM:], prm_d[:, N_LAM:]).then_inc(s_prm, 16)
            sp.dma_start(ddiag[:], ddiag_d).then_inc(s_dd, 16)
            sp.dma_start(col[:], col_d).then_inc(s_col, 16)
            for s in range(2):
                sp.dma_start(raw[:, s, :], panels[s]).then_inc(raw_in[s], 16)
            sp.dma_start(h[:], x_d).then_inc(s_h, 16)

            def toeplitz(o, q):
                wait(sp, k_diag, o + 1)
                wait(sp, zeroed, 3)
                for j in range(J):
                    sp.dma_start(toep[j * C:(j + 1) * C, q, :, :, j * C:].rearrange("p e g n -> p (e g) n"),
                                 k_out[:, :, :, 0:(J - j) * C].rearrange("p e g n -> p (e g) n")
                                 ).then_inc(t_in[q], 16)

            def next_panels():
                for u in (2, 3):
                    wait(sp, w_split, u - 1)
                    sp.dma_start(raw[:, u % 2, :], panels[u]).then_inc(raw_in[u % 2], 16)

            octets(sp, [(toeplitz, 0)], late={NO: next_panels})


            for u in range(4, 8):
                wait(sp, w_split, u - 1)
                sp.dma_start(raw[:, u % 2, :], panels[u]).then_inc(raw_in[u % 2], 16)
            wait(sp, y_lo, KT)
            sp.dma_start(mask[:], mask_d).then_inc(s_mask, 16)
            with sp.Fori(4, NU // 2) as i:
                for s in range(2):
                    sp.wait_ge(w_split, 2 * i + s - 1)
                    sp.sem_inc(passed, 1)
                    sp.dma_start(raw[:, s, :], panels[2 * i + s]).then_inc(raw_in[s], 16)
            for m in range(KT):
                wait(sp, out_t, m + 1)
                sp.dma_start(out_d[m], h[:, m, :]).then_inc(out_s, 16)
            sp.wait_ge(out_s, 16 * KT)

        @block.gpsimd
        def _(pool):
            def gate():
                nc.gpsimd.tensor_tensor(gate_sb[:, 0:1], gate_sb[:, 1:2], gate_sb[:, 1:2], ALU.mult)

            nc.gpsimd.memset(gate_sb[:], 0.0).then_inc(zeroed, 1)
            wait(pool, zeroed, 1)

            nc.gpsimd.memset(st[:], 0.0).then_inc(zeroed, 1)
            nc.gpsimd.memset(toep[:], 0.0).then_inc(zeroed, 1)
            nc.gpsimd.memset(p_0[:], 0.0).then_inc(zeroed, 1)

            def readout(o, q):
                c_re = prm[:, bass.ds(PRM["c_re"][0] + o * OGP * C, OGP * C)].rearrange(
                    "p (g c) -> p g c", c=C).unsqueeze(2).to_broadcast([P, OGP, J + 1, C])
                c_im = prm[:, bass.ds(PRM["c_im"][0] + o * OGP * C, OGP * C)].rearrange(
                    "p (g c) -> p g c", c=C).unsqueeze(2).to_broadcast([P, OGP, J + 1, C])

                def lam(table):
                    return table[:, bass.ds(o * OGP, OGP), 0:J + 1].unsqueeze(3).to_broadcast([P, OGP, J + 1, C])

                wait(pool, w_done, 2 * o)
                gate()
                for i, (c, table) in enumerate(((c_re, l_re), (c_im, nl_im), (c_re, nl_im), (c_im, nl_re))):
                    nc.gpsimd.tensor_tensor(w_tmp[:, i], c, lam(table), ALU.mult).then_inc(w_step, 1)
                pool.wait_ge(w_step, 4 * o + 4)
                wait(pool, k_mm, o)
                wait(pool, w_copied, o)
                wait(pool, st_done, 2 * o - 2)
                gate()
                nc.gpsimd.tensor_tensor(w_k[:], w_tmp[:, 0:3:2], w_tmp[:, 1:4:2], ALU.add).then_inc(w_done, 1)
                r8 = mag[:, bass.ds(o * OGP, OGP), J:J + 1].to_broadcast([P, OGP, NK])
                for ri in range(2):
                    ins = nc.gpsimd.tensor_tensor(decay[:, q, ri], r8,
                                                  C_("keep").unsqueeze(1).to_broadcast([P, OGP, NK]), ALU.mult)
                ins.then_inc(w_done, 1)

            wait(pool, s_cst, 16)
            wait(pool, s_prm, 16)
            wait(pool, setup_v, SETUP_POW)
            wait(pool, setup_a, 3)
            readout(0, 0)
            wait(pool, sq_ready, NO)
            for o in range(NO):
                part = xy[:, o * OCT:(o + 1) * OCT, :]
                nc.gpsimd.tensor_tensor(part, part, PR("g_in")[:, o * OCT:(o + 1) * OCT].unsqueeze(2).to_broadcast(
                    [P, OCT, NK]), ALU.mult).then_inc(u_step, 1)
            readout(1, 1)
            with pool.Fori(1, NO // 2) as i:
                readout(2 * i, 0)
                readout(2 * i + 1, 1)

            wait(pool, w_done, 2 * NO)
            wait(pool, p_done, 2 * NO)

            def split(u, s):
                pool.wait_ge(raw_in[s % 2], 16 * (u // 2 + 1) if isinstance(u, int) else 8 * (u - s) + 16 * (s // 2 + 1))
                wait(pool, unit_done, u - 3)
                gate()
                nc.gpsimd.tensor_scalar(w_hi[:, s, :], raw[:, s % 2, :], 1.0, 0.0, ALU.mult, ALU.add
                                        ).then_inc(w_hi_done, 1)
                pool.wait_ge(w_hi_done, u + 1)
                nc.gpsimd.tensor_tensor(w_lo[:, s, :], raw[:, s % 2, :], w_hi[:, s, :].bitcast(F32),
                                        ALU.subtract).then_inc(w_split, 1)

            for s in range(4):
                split(s, s)
            with pool.Fori(1, NU // 4) as i:
                for s in range(4):
                    split(4 * i + s, s)

        @block.scalar
        def _(a):
            act_fn = nc.scalar.activation

            wait(a, s_lam, 16)
            act_fn(small[:, 0], PR("log_dt"), ACT.Exp).then_inc(setup_a, 1)
            wait(a, setup_v, SETUP_EXP)
            act_fn(small[:, 4], small[:, 3], ACT.Tanh, scale=0.5).then_inc(setup_a, 1)
            act_fn(mag[:], mag[:], ACT.Exp).then_inc(setup_a, 1)
            wait(a, setup_v, SETUP_PH)
            act_fn(l_im[:], ph[:], ACT.Sin, scale=TWO_PI).then_inc(setup_a, 1)
            act_fn(l_re[:], ph[:], ACT.Sin, scale=PI_).then_inc(setup_a, 1)
            for o in range(NO):
                wait(a, s_xu[o // 2], 16)
                wait(a, sq_used, o - 1)
                act_fn(y_sb[:, o % 2, :], xy[:, o * OCT:(o + 1) * OCT, :].rearrange("p g k -> p (g k)"),
                       ACT.Square).then_inc(sq_ready, 1)

            wait(a, setup_v, SETUP_MS)
            act_fn(rstd_u[:, 0], rstd_u[:, 1], ACT.Sqrt).then_inc(setup_a, 1)

            def frame(c):
                wait(a, frame_v, 5 * c + 3)
                pairs = bass.ds(8 * c, 8)
                act_fn(sink_[:, pairs], phk[:], ACT.Sin, scale=TWO_PI).then_inc(frame_a, 1)
                act_fn(cosk[:, pairs], phk[:], ACT.Sin, scale=PI_).then_inc(frame_a, 1)

            def copy_u(o, q):
                wait(a, u_done, o + 1)
                wait(a, y_mm, o - 1)
                act_fn(u_sb[:, q].rearrange("p g k -> p (g k)"),
                       xy[:, bass.ds(o * OCT, OCT), :].rearrange("p g k -> p (g k)"), ACT.Copy).then_inc(u_copied, 1)
                if isinstance(o, int) and o == 0:
                    frame(0)

            def copy_w(o, q):
                wait(a, w_done, 2 * o + 1)
                wait(a, y_mm, o - 1)
                act_fn(w_ri[:, q].rearrange("p r g j c -> p (r g j c)"),
                       w_k[:].rearrange("p r g j c -> p (r g j c)"), ACT.Copy).then_inc(w_copied, 1)

            def evacuate_v(o, q):
                wait(a, t_mm, o + 1)
                act_fn(v_ri[:, q].rearrange("p r g n -> p r (g n)"), ps[:, 0:2, :], ACT.Copy).then_inc(v_evac, 1)

            def evacuate_k(o, q):
                wait(a, k_mm, o + 1)
                wait(a, t_in[1 - q], 16 * J * ((o + 1) // 2))
                for e in range(2):
                    act_fn(k_out[:, e].rearrange("p g n -> p (g n)"), ps[32 * e:32 * e + C, 2, :],
                           ACT.Copy).then_inc(k_evac, 1)

            def copy_p(o, q):
                wait(a, p_done, 2 * o + 2)
                wait(a, zeroed, 4)
                wait(a, k_mm, o)
                for e in range(2):
                    r = slice(64 * e, 64 * e + 64)
                    act_fn(p_0[r, :, :, e, 0:C], p_ri[r, q, :, :, J - 1, :], ACT.Copy).then_inc(p_copied, 1)

            y_rows = y_sb[0:NK].rearrange("p a n -> p (a n)")

            def evacuate_y(o, q):
                wait(a, y_mm, o + 1)
                wait(a, y_turned, o)
                for e in range(2):
                    act_fn(y_rows.rearrange("p (j g e c) -> p e g j c", j=J, g=OGP, e=2)[:, e],
                           ps[0:NK, 5 + e, :].rearrange("p (g j c) -> p g j c", j=J, c=C), ACT.Copy).then_inc(y_evac, 1)

            def gelu(o, q):
                wait(a, y_turned, o + 1)
                act_fn(xy[:, bass.ds(o * OCT, OCT), :].rearrange("p g k -> p (g k)"), ps[:, 7, :],
                       ACT.Gelu_apprx_tanh).then_inc(gelu_done, 1)

            def y_to_hi(o):
                wait(a, gelu_done, o + 1)
                wait(a, st_done, 2 * NO)
                wait(a, w_done, 2 * NO)
                act_fn(hid[:, 0, 0, o, :], xy[:, o * OCT:(o + 1) * OCT, :].rearrange("p g k -> p (g k)"),
                       ACT.Copy).then_inc(y_hi, 1)

            octets(a, [(copy_p, 0), (copy_u, 0), (evacuate_y, 2), (copy_w, 0), (evacuate_k, 0), (evacuate_v, -1),
                       (frame, "begin"), (gelu, 2)],
                   late={NO + 1: lambda: [y_to_hi(o) for o in range(KT - 1)]})

            y_to_hi(KT - 1)

            def norm_hi(added, m, outs):
                wait(a, h_added, added)
                for g, dst in outs:
                    act_fn(dst[:, 0, bass.ds(m, 1), :].rearrange("p a n -> p (a n)"),
                           h[:, bass.ds(m, 1), :].rearrange("p a n -> p (a n)"),
                           ACT.Copy, scale=col[:, bass.ds(COL[g][0] + m, 1)]).then_inc(n_hi, 1)

            def root(n):
                wait(a, stat_v, 2 * n + 2)
                act_fn(rstd[:], stat[:], ACT.Sqrt).then_inc(stat_a, 1)

            wait(a, s_h, 16)
            wait(a, s_col, 16)
            with a.Fori(0, KT // 2) as i:
                for e in range(2):
                    a.wait_ge(unit_done, 4 * i + 2 * e + 2)
                    act_fn(t2[:, e, :], ps[:, 2 * e + 1, :], ACT.Sigmoid,
                           bias=col[:, bass.ds(COL["b_gate"][0] + 2 * i + e, 1)]).then_inc(sig_done, 1)
                    norm_hi(2 * i + e + 1, 2 * i + e, [("g_mlp0", act)])

            def mlp(layer):
                n0 = H_MLP[layer]
                root(0 if layer == 0 else 2)

                def hidden(b, par):
                    for m in range(KT):
                        n = NB_FF * KT * layer + KT * b + m
                        a.wait_ge(hid_sq, n + 1)
                        act_fn(hid[:, par, 0, m, :], t2[:, m % 2, :], ACT.Copy).then_inc(hid_hi, 1)

                with a.Fori(0, NB_FF // 2) as i:
                    hidden(2 * i, 0)
                    hidden(2 * i + 1, 1)
                if layer == 0:
                    with a.Fori(0, KT) as m:
                        norm_hi(n0 + (NB_FF - 1) * KT + 1 + m, m, [("g_kv", act), ("g_q", hid[:, 0])])

            mlp(0)
            root(1)
            wait(a, stat_c, 2)
            act_fn(rcol[:], scol[:], ACT.Sqrt).then_inc(stat_a, 1)

            def stage(Q):
                u, n, q = Q // NBLK, Q % NBLK, Q % 2
                wait(a, q_done, 2 * u + 2)
                wait(a, pads, 1)
                wait(a, s_mm, Q - 1)
                for e in range(2):
                    r = slice(64 * e, 64 * e + 64)
                    act_fn(qstage[r, q, e:e + 3:2, :], qT[r, 2 * u:2 * u + 2, bass.ds(n * BLK, BLK)],
                           ACT.Copy, scale=HD ** -0.5).then_inc(q_staged, 1)

            def exps(Q):
                u, n, q = Q // NBLK, Q % NBLK, Q % 2
                a.wait_ge(m_step, 4 * Q + 4)
                act_fn(es[:, q, :], sm[:, q, :], ACT.Exp).then_inc(es_done, 1)
                for i in range(4):
                    act_fn(s_sb[:, q, i, :], s_sb[:, q, i, :], ACT.Exp, bias=negm[:, q, i:i + 1],
                           accum_out=den[:, q, i:i + 1]).then_inc(p_exp, 1)

            def turned(Q):
                u, n, q = Q // NBLK, Q % NBLK, Q % 2
                a.wait_ge(pt_mm, Q + 1)
                act_fn(pT[:, q, 0:2].rearrange("p i b n -> p (i b n)"), ps[:, 4, :], ACT.Copy).then_inc(pt_a, 1)

            def o_hi(Q):
                u, n, q = Q // NBLK, Q % NBLK, Q % 2
                a.wait_ge(ot_mm, Q + 1)
                act_fn(hid[:, 1, 0, 2 * u:2 * u + 2, bass.ds(n * BLK, BLK)],
                       ps[:, 7, q * 256:q * 256 + 256].rearrange("p (t n) -> p t n", t=2),
                       ACT.Copy).then_inc(ot_hi, 1)

            stage(0)
            skewed([(turned, 2), (stage, -1), (o_hi, 3), (exps, 0)])

            with a.Fori(0, KT) as m:
                norm_hi(H_O + 1 + m, m, [("g_mlp1", act)])
            mlp(1)
            wait(a, stat_c, 4)
            act_fn(rcol[:], scol[:], ACT.Sqrt).then_inc(stat_a, 1)

        @block.vector
        def _(v):
            tt, ts, stt = nc.vector.tensor_tensor, nc.vector.tensor_scalar, nc.vector.scalar_tensor_tensor
            count = [0]

            def link(ins):
                count[0] += 1
                ins.then_inc(setup_v, 1)
                v.wait_ge(setup_v, count[0])

            def sm_(i):
                return small[:, i]

            def turns(dst, tmp):
                link(ts(tmp, dst, ROUND, ROUND, ALU.add, ALU.subtract))
                link(tt(dst, dst, tmp, ALU.subtract))

            nc.vector.memset(acc[:], 0.0).then_inc(sq_acc, 1)
            nc.vector.memset(stat[:], 0.0).then_inc(bank_free, 4)
            wait(v, s_lam, 16)
            wait(v, s_cst, 16)
            re, im = sm_(1), PR("a_im")
            link(ts(re, PR("a_re"), LAM_MAX, None, ALU.min))
            wait(v, setup_a, 1)
            link(tt(sm_(2), im, sm_(0), ALU.mult))
            link(tt(sm_(3), re, sm_(0), ALU.mult))
            power = C_("pow").unsqueeze(1).to_broadcast([P, GP, NPOW])
            link(tt(mag[:], sm_(3).unsqueeze(2).to_broadcast([P, GP, NPOW]), power, ALU.mult))
            assert count[0] == SETUP_EXP
            link(ts(sm_(2), sm_(2), 1.0 / (2.0 * np.pi), None, ALU.mult))
            turns(sm_(2), sm_(5))
            link(tt(ph[:], sm_(2).unsqueeze(2).to_broadcast([P, GP, NPOW]), power, ALU.mult))
            turns(ph[:], rnd[:])
            assert count[0] == SETUP_PH
            link(ts(sm_(6), sm_(2), float(J), None, ALU.mult))
            turns(sm_(6), sm_(5))
            wait(v, setup_a, 5)
            link(ts(sm_(7), sm_(4), -1.0, 1.0, ALU.mult, ALU.add))
            link(nc.vector.reciprocal(sm_(7), sm_(7)))
            link(stt(sm_(7), sm_(4), 2.0, sm_(7), ALU.mult, ALU.mult))
            sh1 = l_re[:, :, 1:2].rearrange("p g a -> p (g a)")
            link(stt(sm_(8), sh1, -2.0, sh1, ALU.mult, ALU.mult))
            link(stt(sm_(9), sm_(8), 1.0, sm_(7), ALU.add, ALU.mult))
            link(tt(sm_(9), sm_(9), sm_(8), ALU.add))
            link(tt(l_re[:], l_re[:], l_re[:], ALU.mult))
            link(ts(l_re[:], l_re[:], -2.0, 1.0, ALU.mult, ALU.add))
            link(tt(l_re[:], l_re[:], mag[:], ALU.mult))
            link(tt(l_im[:], l_im[:], mag[:], ALU.mult))
            link(ts(nl_re[:], l_re[:, :, 0:J + 1], -1.0, None, ALU.mult))
            link(ts(nl_im[:], l_im[:, :, 0:J + 1], -1.0, None, ALU.mult))
            assert count[0] == SETUP_POW
            li1 = l_im[:, :, 1:2].rearrange("p g a -> p (g a)")
            link(tt(sm_(5), re, re, ALU.mult))
            link(tt(sm_(10), im, im, ALU.mult))
            link(tt(sm_(5), sm_(5), sm_(10), ALU.add))
            link(nc.vector.reciprocal(sm_(5), sm_(5)))
            link(tt(sm_(10), sm_(9), re, ALU.mult))
            link(tt(sm_(11), li1, im, ALU.mult))
            link(tt(sm_(10), sm_(10), sm_(11), ALU.add))
            link(tt(sm_(10), sm_(10), sm_(5), ALU.mult))
            link(tt(sm_(12), li1, re, ALU.mult))
            link(tt(sm_(13), sm_(9), im, ALU.mult))
            link(tt(sm_(12), sm_(12), sm_(13), ALU.subtract))
            link(tt(sm_(12), sm_(12), sm_(5), ALU.mult))
            f_re = sm_(10).unsqueeze(2).to_broadcast([P, GP, J])
            f_im = sm_(12).unsqueeze(2).to_broadcast([P, GP, J])
            lr, li = l_re[:, :, J + 1:], l_im[:, :, J + 1:]
            tmp = rnd[:, :, 0:J]
            link(tt(x_re[:], lr, f_re, ALU.mult))
            link(tt(tmp, li, f_im, ALU.mult))
            link(tt(x_re[:], x_re[:], tmp, ALU.subtract))
            link(tt(x_im[:], lr, f_im, ALU.mult))
            link(tt(tmp, li, f_re, ALU.mult))
            link(tt(x_im[:], x_im[:], tmp, ALU.add))

            wait(v, sq_used, NO)
            link(nc.vector.tensor_reduce(rstd_u[:, 0], ps[:, 7, :].rearrange("p (g k) -> p k g", k=NK), AX.X, ALU.add))
            link(ts(rstd_u[:, 0], rstd_u[:, 0], 1.0 / D, EPS, ALU.mult, ALU.add))
            link(nc.vector.reciprocal(rstd_u[:, 1], rstd_u[:, 0]))
            assert count[0] == SETUP_MS
            wait(v, setup_a, 6)
            wait(v, s_dd, 16)
            wait(v, s_prm, 16)

            def frame(c):
                pairs = bass.ds(8 * c, 8)
                wait(v, frame_a, 2 * c)
                tt(phk[:], small[:, 6, pairs].unsqueeze(2).to_broadcast([P, 8, NK]),
                   C_("chunk").unsqueeze(1).to_broadcast([P, 8, NK]), ALU.mult).then_inc(frame_v, 1)
                v.wait_ge(frame_v, 5 * c + 1)
                ts(phr[:], phk[:], ROUND, ROUND, ALU.add, ALU.subtract).then_inc(frame_v, 1)
                v.wait_ge(frame_v, 5 * c + 2)
                tt(phk[:], phk[:], phr[:], ALU.subtract).then_inc(frame_v, 1)

            def frame_end(c):
                pairs = bass.ds(8 * c, 8)
                v.wait_ge(frame_a, 2 * c + 2)
                tt(cosk[:, pairs], cosk[:, pairs], cosk[:, pairs], ALU.mult).then_inc(frame_v, 1)
                v.wait_ge(frame_v, 5 * c + 4)
                ts(cosk[:, pairs], cosk[:, pairs], -2.0, 1.0, ALU.mult, ALU.add).then_inc(frame_v, 1)
                v.wait_ge(frame_v, 5 * c + 5)

            def project(o, q):
                def b(name):
                    return prm[:, bass.ds(PRM[name][0] + o * OGP * C, OGP * C)].rearrange(
                        "p (g c) -> p g c", c=C).unsqueeze(2).to_broadcast([P, OGP, J, C])

                def x(table):
                    return table[:, bass.ds(o * OGP, OGP), :].unsqueeze(3).to_broadcast([P, OGP, J, C])

                wait(v, p_done, 2 * o)
                for i, (bb, xx) in enumerate((("b_re", x_re), ("b_im", x_im), ("b_re", x_im), ("b_im", x_re))):
                    tt(p_tmp[:, i], b(bb), x(xx), ALU.mult).then_inc(p_step, 1)

            def first_frame(o, q):
                if isinstance(o, int) and o == 0:
                    frame(0)

            def project_sum(o, q):
                v.wait_ge(p_step, 4 * o + 4)
                wait(v, t_mm, o - 1)
                wait(v, p_copied, 2 * o - 2)
                tt(p_ri[:, q, 0], p_tmp[:, 0], p_tmp[:, 1], ALU.subtract).then_inc(p_done, 1)
                tt(p_ri[:, q, 1], p_tmp[:, 2], p_tmp[:, 3], ALU.add).then_inc(p_done, 1)

            def inputs(o, q):
                wait(v, u_step, o + 1)
                part = xy[:, bass.ds(o * OCT, OCT), :]
                tt(part, part, rstd_u[:, 0].unsqueeze(1).to_broadcast([P, OCT, NK]), ALU.mult).then_inc(u_done, 1)

            def skip_connection(o):
                wait(v, k_evac, 2 * o + 2)
                tt(k_out[:, :, :, 0:C], k_out[:, :, :, 0:C],
                   ddiag[:, :, bass.ds(o * OGP, OGP), :], ALU.add).then_inc(k_diag, 1)

            def run_states(o, q):
                if isinstance(o, int) and o == 0:
                    frame_end(0)
                skip_connection(o)
                cos = cosk[:, bass.ds(o * OGP, OGP), :].rearrange("p g k -> p (g k)").unsqueeze(1).to_broadcast([P, 2, OGP * NK])
                sin = sink_[:, bass.ds(o * OGP, OGP), :].rearrange("p g k -> p (g k)").unsqueeze(1).to_broadcast([P, 2, OGP * NK])

                def flat(t):
                    return t.rearrange("p r g k -> p r (g k)")

                b = ps[:, 4, :].rearrange("p (r n) -> p r n", r=2)
                wait(v, st_done, 2 * o)
                wait(v, b_mm, o + 1)
                tt(flat(rc[:]), b, cos, ALU.mult).then_inc(rot, 1)
                tt(flat(rs[:]), b, sin, ALU.mult).then_inc(b_read, 1)
                v.wait_ge(rot, 6 * o + 1)
                v.wait_ge(b_read, o + 1)
                tt(rb[:, 0], rc[:, 0], rs[:, 1], ALU.add).then_inc(rot, 1)
                tt(rb[:, 1], rc[:, 1], rs[:, 0], ALU.subtract).then_inc(rot, 1)
                v.wait_ge(rot, 6 * o + 3)
                v.wait_ge(w_done, 2 * o + 2)
                nc.vector.tensor_tensor_scan(rb[:].rearrange("p r g k -> p (r g k)"),
                                             decay[:, q].rearrange("p r g k -> p (r g k)"),
                                             rb[:].rearrange("p r g k -> p (r g k)"),
                                             0.0, ALU.mult, ALU.add).then_inc(rot, 1)
                v.wait_ge(rot, 6 * o + 4)
                tt(flat(rc[:]), flat(rb[:]), cos, ALU.mult).then_inc(rot, 1)
                tt(flat(rs[:]), flat(rb[:]), sin, ALU.mult).then_inc(rot, 1)
                v.wait_ge(rot, 6 * o + 6)
                wait(v, zeroed, 3)
                wait(v, y_mm, o - 1)
                tt(st[:, q, 0, :, 1:], rc[:, 0], rs[:, 1], ALU.subtract).then_inc(st_done, 1)
                tt(st[:, q, 1, :, 1:], rs[:, 0], rc[:, 1], ALU.add).then_inc(st_done, 1)

            octets(v, [(project_sum, -1), (inputs, -1), (first_frame, 0), (frame, "begin"), (project, -2),
                       (frame_end, "end"), (run_states, 0)])

            for o in range(NO):
                wait(v, y_hi, o + 1)
                tt(hid[:, 0, 1, o, :], xy[:, o * OCT:(o + 1) * OCT, :].rearrange("p g k -> p (g k)"),
                   hid[:, 0, 0, o, :].bitcast(F32), ALU.subtract).then_inc(y_lo, 1)

            def tile(t, m):
                return t[:, bass.ds(m, 1), :].rearrange("p a n -> p (a n)")

            def normed(added, norm, n_base, m, outs):
                v.wait_ge(h_added, added)
                tt(t1[:], tile(h, m), tile(h, m), ALU.mult).then_inc(sq_tmp, 1)
                v.wait_ge(sq_tmp, norm * KT + m + 1)
                v.wait_ge(sq_acc, norm * (KT + 1) + m + 1)
                tt(acc[:], acc[:], t1[:], ALU.add).then_inc(sq_acc, 1)
                for i, (g, dst) in enumerate(outs):
                    v.wait_ge(n_hi, n_base + i + 1)
                    stt(tile(dst[:, 1], m), tile(h, m), col[:, bass.ds(COL[g][0] + m, 1)],
                        tile(dst[:, 0], m).bitcast(F32), ALU.mult, ALU.subtract).then_inc(n_lo, 1)

            def inverse(n, cols=False):
                wait(v, stat_mm, n + 1)
                if cols:
                    wait(v, stat_col_mm, 1)
                ts(stat[:], ps[:, 7, :], 1.0 / D, EPS, ALU.mult, ALU.add).then_inc(stat_v, 1)
                if cols:
                    ts(scol[:], ps[:, 6, 0:NBLK], 1.0 / D, EPS, ALU.mult, ALU.add).then_inc(stat_c, 1)
                wait(v, stat_v, 2 * n + 1)
                nc.vector.reciprocal(stat[:], stat[:]).then_inc(stat_v, 1)
                nc.vector.memset(acc[:], 0.0).then_inc(sq_acc, 1)
                if cols:
                    v.wait_ge(stat_c, 1)
                    nc.vector.reciprocal(scol[:], scol[:]).then_inc(stat_c, 1)

            wait(v, s_h, 16)
            wait(v, s_col, 16)
            with v.Fori(0, KT // 2) as i:
                for e in range(2):
                    m = 2 * i + e
                    v.wait_ge(sig_done, m + 1)
                    v.wait_ge(sq_acc, m + 1)
                    stt(t1[:], ps[:, 2 * e, :], col[:, bass.ds(COL["b_val"][0] + m, 1)], t2[:, e, :],
                        ALU.add, ALU.mult).then_inc(bank_free, 2)
                    v.wait_ge(bank_free, 4 + 2 * m + 2)
                    hv = tile(h, m).rearrange("p (k j) -> p j k", j=J)
                    tt(hv, t1[:].rearrange("p (j k) -> p j k", j=J), hv, ALU.add).then_inc(h_added, 1)
                    normed(m + 1, 0, m, m, [("g_mlp0", act)])

            def mlp(layer):
                base, n0, norm = U_MLP[layer], H_MLP[layer], 2 * layer
                inverse(norm)
                wait(v, stat_a, STAT_A[norm])

                def hidden(b, par):
                    for m in range(KT):
                        U = base + m + (0 if isinstance(b, int) and b == 0 else 2 * KT * b - KT)
                        n = NB_FF * KT * layer + KT * b + m
                        v.wait_ge(unit_done, U + 1)
                        stt(t1[:], ps[:, m % 4, :], 0.0, rstd[:], ALU.max, ALU.mult).then_inc(bank_free, 1)
                        v.wait_ge(bank_free, 4 + U + 1)
                        tt(t2[:, m % 2, :], t1[:], t1[:], ALU.mult).then_inc(hid_sq, 1)
                        v.wait_ge(hid_hi, n + 1)
                        tt(hid[:, par, 1, m, :], t2[:, m % 2, :], hid[:, par, 0, m, :].bitcast(F32),
                           ALU.subtract).then_inc(hid_lo, 1)

                def output(b, last):
                    U0 = base + 2 * KT * b + (KT if last else 2 * KT)
                    a0 = n0 + KT * b
                    with v.Fori(0, KT // 4) as i:
                        for s in range(4):
                            m = 4 * i + s
                            v.wait_ge(unit_done, U0 + 1 + m)
                            v.wait_ge(h_added, a0 + m)
                            tt(tile(h, m), ps[:, s, :], tile(h, m), ALU.add).then_inc(bank_free, 1)
                            v.wait_ge(bank_free, 4 + U0 + 1 + m)
                            v.sem_inc(h_added, 1)
                            if last and layer == 0:
                                normed(a0 + m + 1, 1, KT + 2 * m, m, [("g_kv", act), ("g_q", hid[:, 0])])
                            elif last:
                                normed(a0 + m + 1, 3, 4 * KT, m, [])

                hidden(0, 0)
                with v.Fori(0, NB_FF // 2 - 1) as i:
                    hidden(2 * i + 1, 1)
                    output(2 * i, False)
                    hidden(2 * i + 2, 0)
                    output(2 * i + 1, False)
                hidden(NB_FF - 1, 1)
                output(NB_FF - 2, False)
                output(NB_FF - 1, True)

            mlp(0)

            inverse(1, cols=True)
            wait(v, stat_a, STAT_A[1])
            nc.vector.memset(kT[:, :, 0:BLK], 0.0).then_inc(pads, 1)
            nc.vector.memset(v_sb[:, 0, :], 0.0).then_inc(pads, 1)
            for t in range(2):
                wait(v, unit_done, U_KV + t + 1)
                wait(v, kv_done, t)
                tt(t1[:], ps[:, t, :], rstd[:], ALU.mult).then_inc(bank_free, 1)
                wait(v, bank_free, 4 + U_KV + t + 1)
                ts(kT[:, t, BLK:], t1[:], COLS("b_k")[:, t:t + 1], None, ALU.add).then_inc(kv_done, 1)
            wait(v, unit_done, U_KV + 4)
            for n in range(NBLK):
                stt(v_sb[:, 1 + n, :], ps[:, 2 + n // 2, (n % 2) * 2 * P:(n % 2 + 1) * 2 * P], rcol[:, n:n + 1],
                    COLS("b_v"), ALU.mult, ALU.add).then_inc(kv_done, 1)
            v.wait_ge(kv_done, 2 + NBLK)
            v.sem_inc(bank_free, 2)
            wait(v, kv_done, 2 + NBLK)
            nc.vector.memset(qstage[:], 0.0).then_inc(pads, 1)

            def queries(m):
                v.wait_ge(unit_done, U_Q + 1 + m)
                tt(t1[:], ps[:, 2 + m % 2, :], rstd[:], ALU.mult).then_inc(bank_free, 1)
                v.wait_ge(bank_free, 4 + U_Q + 1 + m)
                ts(qT[:, m, :], t1[:], COLS("b_q")[:, m:m + 1], None, ALU.add).then_inc(q_done, 1)
                v.wait_ge(q_done, m + 1)

            queries(0)
            queries(1)
            wait(v, s_mask, 16)

            def maxima(Q):
                u, n, q = Q // NBLK, Q % NBLK, Q % 2
                sink = COLS("sink")[:, 4 * u:4 * u + 4]
                v.wait_ge(s_mm, Q + 1)
                tt(s_sb[:, q], ps[:, 0:2, :].rearrange("p a (i n) -> p (a i) n", n=2 * BLK),
                   mask[:, bass.ds(n, 1), :].to_broadcast([P, 4, 2 * BLK]), ALU.add).then_inc(s_masked, 1)
                v.wait_ge(s_masked, Q + 1)
                nc.vector.tensor_reduce(mx[:, q], s_sb[:, q], AX.X, ALU.max).then_inc(m_step, 1)
                v.wait_ge(m_step, 4 * Q + 1)
                tt(mx[:, q], mx[:, q], sink, ALU.max).then_inc(m_step, 1)
                v.wait_ge(m_step, 4 * Q + 2)
                ts(negm[:, q], mx[:, q], -1.0, None, ALU.mult).then_inc(m_step, 1)
                tt(sm[:, q], sink, mx[:, q], ALU.subtract).then_inc(m_step, 1)

            def denominators(Q):
                u, n, q = Q // NBLK, Q % NBLK, Q % 2
                v.wait_ge(p_exp, 4 * Q + 4)
                tt(den[:, q], den[:, q], es[:, q], ALU.add).then_inc(den_done, 1)
                v.wait_ge(den_done, Q + 1)
                nc.vector.reciprocal(rden[:, q], den[:, q]).then_inc(rden_done, 1)

            def turned(Q):
                u, n, q = Q // NBLK, Q % NBLK, Q % 2
                v.wait_ge(pt_mm, Q + 1)
                ts(pT[:, q, 2:4].rearrange("p i b n -> p (i b n)"), ps[:, 5, :], 1.0, None, ALU.mult).then_inc(pt_v, 1)

            def normalize(Q):
                u, n, q = Q // NBLK, Q % NBLK, Q % 2
                v.wait_ge(o_mm, Q + 1)
                v.wait_ge(rden_done, Q + 1)
                tt(o_sb[:, q], ps[:, 6, q * 256:q * 256 + 256].rearrange("p (i d) -> p i d", d=HD),
                   rden[:, q].unsqueeze(2).to_broadcast([P, 4, HD]), ALU.mult).then_inc(o_norm, 1)

            def o_low(Q):
                u, n, q = Q // NBLK, Q % NBLK, Q % 2
                v.wait_ge(ot_hi, Q + 1)
                tt(hid[:, 1, 1, 2 * u:2 * u + 2, bass.ds(n * BLK, BLK)],
                   ps[:, 7, q * 256:q * 256 + 256].rearrange("p (t n) -> p t n", t=2),
                   hid[:, 1, 0, 2 * u:2 * u + 2, bass.ds(n * BLK, BLK)].bitcast(F32),
                   ALU.subtract).then_inc(ot_lo, 1)

            def next_queries(Q):
                if Q % 2 == 0 and 2 + Q // 2 < KT:
                    queries(2 + Q // 2)

            skewed([(turned, 2), (maxima, 0), (normalize, 2), (denominators, 1), (o_low, 3), (next_queries, 0)])

            with v.Fori(0, KT // 4) as i:
                for s in range(4):
                    m = 4 * i + s
                    v.wait_ge(unit_done, U_O + 1 + m)
                    stt(tile(h, m), ps[:, (s + 2) % 4, :], col[:, bass.ds(COL["b_o"][0] + m, 1)], tile(h, m),
                        ALU.add, ALU.add).then_inc(bank_free, 1)
                    v.wait_ge(bank_free, 4 + U_O + 1 + m)
                    v.sem_inc(h_added, 1)
                    normed(H_O + m + 1, 2, 3 * KT + m, m, [("g_mlp1", act)])

            mlp(1)
            wait(v, stat_col_mm, 2)
            ts(scol[:], ps[:, 6, 0:NBLK], 1.0 / D, EPS, ALU.mult, ALU.add).then_inc(stat_c, 1)
            v.wait_ge(stat_c, 3)
            nc.vector.reciprocal(scol[:], scol[:]).then_inc(stat_c, 1)
            wait(v, stat_a, STAT_A[3])
            tt(t2[:, 0].rearrange("p (n t) -> p n t", n=NBLK), ident.unsqueeze(1).to_broadcast([P, NBLK, P]),
               rcol[:].unsqueeze(2).to_broadcast([P, NBLK, P]), ALU.mult).then_inc(diagonals, 1)
            wait(v, stat_mm, 4)
            for m in range(KT):
                stt(h[:, m, :], h[:, m, :], COLS("g_out")[:, m:m + 1], ps[:, 7, :], ALU.mult, ALU.mult).then_inc(out_t, 1)

        @block.tensor
        def _(pe):
            mm, turn = nc.tensor.matmul, nc.tensor.transpose

            wait(pe, s_cst, 16)
            for o in range(NO):
                wait(pe, sq_ready, o + 1)
                mm(ps[:, 7, :], C_("same_step"), y_sb[:, o % 2, :], start=(o == 0), stop=(o == NO - 1)
                   ).then_inc(sq_used, 1)

            def fold(o, q):
                wait(pe, p_done, 2 * o + 2)
                wait(pe, v_evac, o)
                for ri in range(2):
                    for g in range(OGP):
                        last = turn(ps[:, ri, g * P:(g + 1) * P], p_ri[:, q, ri, g].rearrange("p j c -> p (j c)"), ident)
                last.then_inc(t_mm, 1)

            def sums(o, q):
                wait(pe, v_evac, o + 1)
                wait(pe, u_copied, o + 1)
                wait(pe, b_read, o)
                for g in range(OGP):
                    for e in range(2):
                        for ri in range(2):
                            last = mm(ps[64 * e:64 * e + 64, 4, (ri * OGP + g) * NK:(ri * OGP + g + 1) * NK],
                                      v_ri[:, q, ri, g, 64 * e:64 * e + 64], u_sb[:, q, 2 * g + e, :],
                                      start=True, stop=True)
                last.then_inc(b_mm, 1)

            def lags(o, q):
                wait(pe, w_done, 2 * o + 1)
                wait(pe, p_copied, 2 * o + 2)
                wait(pe, k_evac, 2 * o)
                pe.sem_inc(passed, 1)
                for g in range(OGP):
                    for ri in range(2):
                        last = mm(ps[0:64, 2, g * P:(g + 1) * P], p_0[:, ri, g].rearrange("p e c -> p (e c)"),
                                  w_k[:, ri, g, 0:J, :].rearrange("p j c -> p (j c)"), start=(ri == 0), stop=(ri == 1))
                last.then_inc(k_mm, 1)

            def outputs(o, q):
                wait(pe, t_in[q], 16 * J * (o // 2 + 1))
                wait(pe, st_done, 2 * o + 2)
                wait(pe, w_copied, o + 1)
                wait(pe, y_evac, 2 * o)
                for g in range(OGP):
                    for e in range(2):
                        r = slice(64 * e, 64 * e + 64)
                        gg = 2 * g + e
                        out = ps[0:NK, 5 + e, g * P:(g + 1) * P]
                        mm(out, u_sb[:, q, gg, :], toep[:, q, e, g, :], start=True, stop=False)
                        for ri in range(2):
                            last = mm(out, st[r, q, ri, g, 0:NK],
                                      w_ri[r, q, ri, g, 1:J + 1, :].rearrange("p j c -> p (j c)"),
                                      start=False, stop=(ri == 1))
                last.then_inc(y_mm, 1)

            def turn_y(o, q):
                wait(pe, y_evac, 2 * o + 2)
                wait(pe, gelu_done, o)
                pe.sem_inc(passed, 1)
                for j in range(J):
                    last = turn(ps[:, 7, j * NK:(j + 1) * NK],
                                y_sb[0:NK].rearrange("p a n -> p (a n)")[:, j * P:(j + 1) * P], ident[0:NK, 0:NK])
                last.then_inc(y_turned, 1)

            def paired(U, s, x, ready, tiles=range(KT)):
                if tiles[0] == 0:
                    pe.wait_ge(w_split, U + 2)
                    pe.wait_ge(bank_free, U + 2)
                for k in tiles:
                    wait(pe, ready[0], ready[1] + k)
                    w = slice(k * P, (k + 1) * P)
                    for b in (s, s + 1):
                        mm(ps[:, b, :], w_hi[:, b, w], x[:, 0, k, :], start=(k == 0), stop=False)
                        mm(ps[:, b, :], w_hi[:, b, w], x[:, 1, k, :], start=False, stop=False)
                        last = mm(ps[:, b, :], w_lo[:, b, w], x[:, 0, k, :], start=False, stop=(k == KT - 1))
                        if k == KT - 1:
                            last.then_inc(unit_done, 1)

            def first_glu_units():
                wait(pe, v_evac, NO)
                paired(U_GLU, 0, hid[:, 0], (y_lo, 1), range(3))

            octets(pe, [(lags, 0), (sums, 0), (fold, -1), (turn_y, 2), (outputs, 1)], late={NO + 1: first_glu_units})

            def unit(U, s, x, ready=None, tiles=range(KT), bank=None, free=None):
                bank = s if bank is None else bank
                if tiles[0] == 0:
                    pe.wait_ge(w_split, U + 1)
                    pe.wait_ge(*(free or (bank_free, U + 1)))
                for k in tiles:
                    if ready is not None:
                        wait(pe, ready[0], ready[1] + ready[2] * k)
                    w = slice(k * P, (k + 1) * P)
                    mm(ps[:, bank, :], w_hi[:, s, w], x[:, 0, k, :], start=(k == 0), stop=False)
                    mm(ps[:, bank, :], w_hi[:, s, w], x[:, 1, k, :], start=False, stop=False)
                    last = mm(ps[:, bank, :], w_lo[:, s, w], x[:, 0, k, :], start=False, stop=(k == KT - 1))
                if tiles[-1] == KT - 1:
                    last.then_inc(unit_done, 1)

            def units(n, U0, x, ready=None):
                with pe.Fori(0, n // 4) as i:
                    for s in range(4):
                        unit(U0 + 4 * i + s, s, x, ready)

            def stats(norm):
                wait(pe, sq_acc, (norm + 1) * (KT + 1))
                mm(ps[:, 7, :], ones, acc[:], start=True, stop=True).then_inc(stat_mm, 1)

            def column_stats():
                for n in range(NBLK):
                    last = mm(ps[:, 6, n:n + 1], acc[:, n * P:(n + 1) * P], ones[:, 0:1], start=True, stop=True)
                last.then_inc(stat_col_mm, 1)

            def mlp(layer):
                base = U_MLP[layer]
                n_lo0 = 0 if layer == 0 else 3 * KT
                paired(base, 0, act, (n_lo, n_lo0 + 1))
                stats(2 * layer)
                paired(base + 2, 2, act, (n_lo, n_lo0 + 1))
                units(4, base + 4, act)

                def second(b, U0, par):
                    pe.wait_ge(hid_lo, NB_FF * KT * layer + KT * b + KT)
                    units(KT, U0, hid[:, par])

                with pe.Fori(0, NB_FF // 2 - 1) as i:
                    units(KT, base + KT + 4 * KT * i, act)
                    second(2 * i, base + 2 * KT + 4 * KT * i, 0)
                    units(KT, base + 3 * KT + 4 * KT * i, act)
                    second(2 * i + 1, base + 4 * KT + 4 * KT * i, 1)
                units(KT, base + (2 * NB_FF - 3) * KT, act)
                second(NB_FF - 2, base + (2 * NB_FF - 2) * KT, 0)
                second(NB_FF - 1, base + (2 * NB_FF - 1) * KT, 1)

            paired(U_GLU, 0, hid[:, 0], (y_lo, 1), range(3, KT))
            paired(U_GLU + 2, 2, hid[:, 0], (y_lo, 1))
            units(2 * KT - 4, U_GLU + 4, hid[:, 0])
            mlp(0)

            for t in range(2):
                unit(U_KV + t, t, act, (n_lo, KT + 1, 2))
                if t == 0:
                    stats(1)
                    column_stats()
            wait(pe, w_split, U_KV + 4)
            wait(pe, bank_free, U_KV + 4)
            for n in range(NBLK):
                tok = slice(n * P, (n + 1) * P)
                out = ps[:, 2 + n // 2, (n % 2) * 2 * P:(n % 2 + 1) * 2 * P].rearrange("p (a m) -> p a m", a=2)
                for k in range(KT):
                    w = slice(k * P, (k + 1) * P)
                    mm(out, act[:, 0, k, tok], w_hi[:, 2:4, w], start=(k == 0), stop=False)
                    mm(out, act[:, 0, k, tok], w_lo[:, 2:4, w], start=False, stop=False)
                    last = mm(out, act[:, 1, k, tok], w_hi[:, 2:4, w], start=False, stop=(k == KT - 1))
            last.then_inc(unit_done, 2)

            def query_unit(m, tiles):
                unit(U_Q + m, m % 4, hid[:, 0], (n_lo, KT + 2, 2), tiles, bank=2 + m % 2,
                     free=(bank_free, U_Q + m + 3))

            def out_unit(m, tiles):
                free = ((bank_free, U_O + m + 3), (bank_free, U_O + m + 3), (s_masked, QUADS * NBLK),
                        (s_masked, QUADS * NBLK))[m]
                wait(pe, ot_lo, NBLK * (tiles[-1] // 2 + 1))
                unit(U_O + m, m, hid[:, 1], None, tiles, bank=(m + 2) % 4, free=free)

            first_half, second_half = range(0, KT // 2), range(KT // 2, KT)
            query_unit(0, range(KT))
            query_unit(1, range(KT))
            query_unit(2, first_half)

            def scores(Q):
                u, n, q = Q // NBLK, Q % NBLK, Q % 2
                wait(pe, q_staged, 2 * Q + 2)
                wait(pe, s_masked, Q)
                wait(pe, kv_done, 2 + NBLK)
                wait(pe, pads, 3)
                wait(pe, bank_free, 4 + U_Q)
                for i in range(4):
                    last = mm(ps[:, i // 2, (i % 2) * 2 * BLK:(i % 2 + 1) * 2 * BLK], qstage[:, q, i, :],
                              kT[:, u // 2, bass.ds(n * BLK, 2 * BLK)], start=True, stop=True)
                last.then_inc(s_mm, 1)

            def turn_p(Q):
                u, n, q = Q // NBLK, Q % NBLK, Q % 2
                pe.wait_ge(p_exp, 4 * Q + 4)
                wait(pe, pt_a, Q)
                wait(pe, pt_v, Q)
                for i in range(4):
                    for b in range(2):
                        at = (i % 2) * 2 * BLK + b * BLK
                        last = turn(ps[:, 4 + i // 2, at:at + BLK], s_sb[:, q, i, b * BLK:(b + 1) * BLK], ident)
                last.then_inc(pt_mm, 1)

            def mix(Q):
                u, n, q = Q // NBLK, Q % NBLK, Q % 2
                pe.wait_ge(pt_a, Q + 1)
                pe.wait_ge(pt_v, Q + 1)
                wait(pe, o_norm, Q)
                for i in range(4):
                    kvh = 2 * (u // 2) + i % 2
                    for b in range(2):
                        last = mm(ps[:, 6, q * 256 + i * HD:q * 256 + (i + 1) * HD], pT[:, q, i, b, :],
                                  v_sb[:, bass.ds(n + b, 1), kvh * HD:(kvh + 1) * HD].rearrange("p a d -> p (a d)"),
                                  start=(b == 0), stop=(b == 1))
                last.then_inc(o_mm, 1)

            def turn_o(Q):
                u, n, q = Q // NBLK, Q % NBLK, Q % 2
                pe.wait_ge(o_norm, Q + 1)
                wait(pe, ot_lo, Q)
                for t in range(2):
                    last = turn(ps[:, 7, q * 256 + t * P:q * 256 + (t + 1) * P],
                                o_sb[:, q, 2 * t:2 * t + 2, :].rearrange("p e d -> p (e d)"), ident)
                last.then_inc(ot_mm, 1)

            early, middle = range(0, 4), range(4, 6)
            beside = {Q: [(query_unit, 2 + (Q + 1) // 2, first_half if Q % 2 else second_half)]
                      for Q in range(2 * (KT - 2) - 1)}
            last_quad = QUADS * NBLK - 1
            beside[last_quad - 4] = [(out_unit, 0, early)]
            beside[last_quad - 3] = [(out_unit, 1, early)]
            beside[last_quad + 1] = [(out_unit, 2, early), (out_unit, 0, middle)]
            beside[last_quad + 2] = [(out_unit, 3, early), (out_unit, 1, middle)]
            beside[last_quad + 3] = [(out_unit, 2, middle), (out_unit, 3, middle)]

            def dense(Q):
                for work, m, tiles in beside.get(Q, []):
                    work(m, tiles)

            skewed([(scores, 0), (dense, None), (mix, 2), (turn_o, 3), (turn_p, 1)])

            for m in range(4):
                out_unit(m, range(6, KT))
            for m in range(4, KT):
                unit(U_O + m, m % 4, hid[:, 1], bank=(m + 2) % 4)
            pe.wait_ge(bank_free, 4 + U_O + KT)
            mlp(1)
            wait(pe, sq_acc, 4 * (KT + 1))
            column_stats()
            wait(pe, diagonals, 1)
            mm(ps[:, 7, :], ones, t2[:, 0, :], start=True, stop=True).then_inc(stat_mm, 1)


def skewed(stages):
    last = QUADS * NBLK
    longest = max(lag for _, lag in stages if lag is not None)
    for Q in range(last + longest):
        for stage, lag in stages:
            if lag is None:
                stage(Q)
            elif 0 <= Q - lag < last:
                stage(Q - lag)


def _feature_rows(a):
    return a.T.reshape(KT, P, L).transpose(1, 0, 2)


def _panels(w):
    n = w.shape[1] // P
    return w.reshape(KT, P, n, P).transpose(2, 1, 0, 3).reshape(n, P, KT * P)


def kernel(**inputs):
    from concourse import bacc
    from concourse.bass_utils import run_bass_kernel_spmd

    f = {k: np.asarray(v) for k, v in inputs.items()}
    x = f["x"][0]

    def states(a):
        a = a.reshape((GP, 2, S) + a.shape[2:])
        return np.moveaxis(a, 0, 2).reshape((P, GP) + a.shape[3:])

    def cols(a):
        return a.reshape(-1, P).T

    def rows(a):
        return np.broadcast_to(a, (P, a.size))

    group = NQ // NKV
    heads = [(2 * (t // group) + e) * group + t % group for t in range(NQ // 2) for e in range(2)]

    panels = []
    glu = _panels(f["s5_w_glu"][0])
    for m in range(KT):
        panels += [glu[m], glu[KT + m]]

    def mlp(layer):
        w_in = _panels(f["w_mlp_in"][layer])
        w_out = [_panels(f["w_mlp_out"][layer][b * D:(b + 1) * D]) for b in range(NB_FF)]
        order = [w_in[0:KT]]
        for b in range(1, NB_FF):
            order += [w_in[b * KT:(b + 1) * KT], w_out[b - 1]]
        order.append(w_out[NB_FF - 1])
        return [p for block in order for p in block]

    panels += mlp(0)
    panels += list(_panels(f["w_kv"]))
    panels += list(_panels(f["w_q"][0].reshape(D, NQ, HD)[:, heads].reshape(D, D)))
    panels += list(_panels(f["w_o"][0].reshape(NQ, HD, D)[heads].reshape(D, D)))
    panels += mlp(1)

    g_in = np.broadcast_to(f["norm_mix"][0].reshape(G, C).T[None], (J, C, G)).reshape(P, G)
    prm = np.concatenate([
        states(f["s5_a_re"][0]), states(f["s5_a_im"][0]),
        states(np.broadcast_to(f["s5_log_dt"][0][:, None], (G, S))),
        states(f["s5_b_re"][0]).reshape(P, -1), states(f["s5_b_im"][0]).reshape(P, -1),
        states(f["s5_c_re"][0].transpose(0, 2, 1)).reshape(P, -1),
        states(f["s5_c_im"][0].transpose(0, 2, 1)).reshape(P, -1), g_in], axis=1)
    skip = f["s5_d"][0].reshape(GP, 2, C)
    ddiag = np.zeros((C, 2, GP, C), np.float32)
    for c in range(C):
        ddiag[c, :, :, c] = skip[:, :, c].T
    b_kv, b_glu = f["b_kv"], f["s5_b_glu"][0]
    col = np.concatenate([
        cols(b_glu[:D]), cols(b_glu[D:]), cols(f["norm_mlp"][0]), cols(f["norm_kv"]), cols(f["norm_mix"][1]),
        cols(f["norm_mlp"][1]), cols(f["norm_final"]), cols(b_kv[:NKV * HD]),
        cols(f["b_q"][0].reshape(NQ, HD)[heads].reshape(-1)), cols(f["b_o"][0]), rows(b_kv[NKV * HD:]),
        rows(f["sinks"][0][heads])], axis=1)

    keep = np.ones(NK)
    keep[0] = 0
    step = np.arange(P) // C
    cst = np.concatenate([
        rows(np.concatenate([np.arange(J + 1), np.arange(J)[::-1]])), rows(np.arange(NK)), rows(keep),
        step[:, None] == step[None, :], np.eye(P), np.ones((P, P))], axis=1).astype(np.float32)
    back = np.arange(BLK)[:, None] + BLK - np.arange(2 * BLK)[None, :]
    inside = (back >= 0) & (back < BLK)
    first = inside & (np.arange(2 * BLK) >= BLK)[None, :]
    mask = np.where(np.stack([first] + [inside] * (NBLK - 1), axis=1), 0.0, -1e30).astype(np.float32)

    arrays = {
        "panels": np.stack(panels),
        "xu": x.reshape(NK, J, G, C).transpose(1, 3, 2, 0).reshape(P, G, NK),
        "x_rows": _feature_rows(x), "prm": prm, "ddiag": ddiag, "cst": cst, "mask": mask, "col": col,
    }
    arrays = {k + "_in": np.ascontiguousarray(v) for k, v in arrays.items()}
    nc = bacc.Bacc("TRN2", target_bir_lowering=False, num_devices=1)
    aps = [nc.dram_tensor(k, v.shape, F32, kind="ExternalInput").ap() for k, v in arrays.items()]
    out = nc.dram_tensor("out", (KT, P, L), F32, kind="ExternalOutput").ap()
    build(nc, *aps, out)
    r = run_bass_kernel_spmd(nc, [arrays], core_ids=[0])
    return r.results[0]["out"].transpose(2, 0, 1).reshape(1, L, D)
```
